# Optimizing a Trainium2 kernel written in Bass

```python
import math
import jax, jax.numpy as jnp
from jax import lax
import numpy as np

D_MODEL = 1024
BATCH = 1
SEQ = 512
DEPTH = 1

HEAD_DIM = 64
DILATIONS = (1, 4, 16)
KEYS_PER_QUERY = 128
WINDOWS = tuple(KEYS_PER_QUERY * d for d in DILATIONS)
N_GROUPS = len(DILATIONS)
HEADS_PER_GROUP = 4
ATT_HEADS = N_GROUPS * HEADS_PER_GROUP
ATT_WIDTH = ATT_HEADS * HEAD_DIM
ATT_OUT_WIDTH = HEADS_PER_GROUP * HEAD_DIM
QUERY_BLOCK = 64
N_BUCKETS = 32
MAX_DISTANCE = WINDOWS[-1]
RWKV_HEADS = D_MODEL // HEAD_DIM
RWKV_WIDTH = RWKV_HEADS * HEAD_DIM
DECAY_LORA = 64
ICLR_LORA = 64
GATE_LORA = 128
RWKV_COLS = 3 * RWKV_WIDTH + DECAY_LORA + ICLR_LORA + GATE_LORA
N_BRANCHES = 2
IN_COLS = 3 * ATT_WIDTH + RWKV_COLS + N_BRANCHES * D_MODEL
D_FF = 4 * D_MODEL
NORM_EPS = 1e-6
LN_X_EPS = 64e-5
L2_EPS = 1e-12


def rmsnorm(x, g):
    xf = x.astype(jnp.float32)
    y = xf * lax.rsqrt(jnp.mean(xf * xf, axis=-1, keepdims=True) + NORM_EPS)
    return (y * g.astype(jnp.float32)).astype(x.dtype)

def t5_bucket(dist):
    max_exact = N_BUCKETS // 2
    d_f = jnp.maximum(dist, 1).astype(jnp.float32)
    large = max_exact + (jnp.log(d_f / max_exact) / math.log(MAX_DISTANCE / max_exact)
                         * (N_BUCKETS - max_exact)).astype(jnp.int32)
    large = jnp.minimum(large, N_BUCKETS - 1)
    return jnp.where(dist < max_exact, dist, large)

def dilated_window_attention(q, k, v, rel_bias):
    b, s = q.shape[0], q.shape[1]
    dil = jnp.array(DILATIONS, jnp.int32)
    dist = dil[:, None] * jnp.arange(KEYS_PER_QUERY + 1, dtype=jnp.int32)[None, :]
    bucket = t5_bucket(dist)
    bias = rel_bias.reshape(N_BUCKETS, N_GROUPS, HEADS_PER_GROUP)[bucket, jnp.arange(N_GROUPS)[:, None]]
    bias = jnp.transpose(bias, (0, 2, 1)).astype(jnp.float32)
    qg = jnp.moveaxis(q, 2, 0)
    kg = jnp.moveaxis(k, 2, 0)
    vg = jnp.moveaxis(v, 2, 0)
    scale = HEAD_DIM ** -0.5

    def one_block(blk):
        start = blk * QUERY_BLOCK
        t = start + jnp.arange(QUERY_BLOCK, dtype=jnp.int32)
        pos = t[None, :, None] - dist[:, None, :]
        valid = pos >= 0
        pos = jnp.maximum(pos, 0)
        qb = lax.dynamic_slice_in_dim(qg, start, QUERY_BLOCK, axis=2)
        kb = jax.vmap(lambda a, p: a[:, p])(kg, pos)
        vb = jax.vmap(lambda a, p: a[:, p])(vg, pos)
        logits = jnp.einsum('gbqhd,gbqjhd->gbhqj', qb, kb,
                            preferred_element_type=jnp.float32) * scale
        logits = logits + bias[:, None, :, None, :]
        logits = jnp.where(valid[:, None, None, :, :], logits, -jnp.inf)
        lse = jax.nn.logsumexp(logits, axis=-1)
        p = jnp.exp(logits - lse[..., None])
        o = jnp.einsum('gbhqj,gbqjhd->gbqhd', p, vb.astype(jnp.float32))
        w_mix = jax.nn.softmax(lse, axis=0)
        o = jnp.einsum('gbhq,gbqhd->bqhd', w_mix, o)
        return o.astype(v.dtype)

    out = lax.map(one_block, jnp.arange(s // QUERY_BLOCK, dtype=jnp.int32))
    return jnp.moveaxis(out, 0, 1).reshape(b, s, ATT_OUT_WIDTH)

def token_shift(f, mu):
    f_prev = jnp.pad(f, ((0, 0), (1, 0), (0, 0)))[:, :-1]
    return f + (f_prev - f) * mu

def rwkv7_time_mix(f, w0, w_w2, a0, w_a2, w_g2, k_k, k_a, r_k, ln_w, ln_b):
    b, s, _ = f.shape
    splits = [RWKV_WIDTH, 2 * RWKV_WIDTH, 3 * RWKV_WIDTH,
              3 * RWKV_WIDTH + DECAY_LORA, 3 * RWKV_WIDTH + DECAY_LORA + ICLR_LORA]
    r, k, v, fw, fa, fg = jnp.split(f, splits, axis=-1)
    w = -jax.nn.softplus(-(w0 + jnp.tanh(fw) @ w_w2)) - 0.5
    decay = jnp.exp(-jnp.exp(w.astype(jnp.float32)))
    a = jax.nn.sigmoid(a0 + fa @ w_a2)
    g = jax.nn.sigmoid(fg) @ w_g2
    kk = (k * k_k).reshape(b, s, RWKV_HEADS, HEAD_DIM).astype(jnp.float32)
    kk = kk / jnp.maximum(jnp.linalg.norm(kk, axis=-1, keepdims=True), L2_EPS)
    k = k * (1 + (a - 1) * k_a)
    heads = lambda t: t.reshape(b, s, RWKV_HEADS, HEAD_DIM).astype(jnp.float32)
    r, k, v, decay, a = heads(r), heads(k), heads(v), heads(decay), heads(a)

    def step(state, inp):
        r_t, w_t, k_t, v_t, kk_t, a_t = inp
        sa = jnp.einsum('bhij,bhj->bhi', state, -kk_t)
        state = (state * w_t[:, :, None, :]
                 + sa[..., None] * (kk_t * a_t)[:, :, None, :]
                 + v_t[..., None] * k_t[:, :, None, :])
        y_t = jnp.einsum('bhij,bhj->bhi', state, r_t)
        return state, y_t

    xs = tuple(jnp.moveaxis(t, 1, 0) for t in (r, decay, k, v, kk, a))
    state0 = jnp.zeros((b, RWKV_HEADS, HEAD_DIM, HEAD_DIM), jnp.float32)
    _, y = lax.scan(step, state0, xs)
    y = jnp.moveaxis(y, 0, 1)
    mu = jnp.mean(y, axis=-1, keepdims=True)
    var = jnp.mean(jnp.square(y - mu), axis=-1, keepdims=True)
    y = ((y - mu) * lax.rsqrt(var + LN_X_EPS)).reshape(b, s, RWKV_WIDTH)
    y = y * ln_w.astype(jnp.float32) + ln_b.astype(jnp.float32)
    bonus = jnp.sum(r * k * r_k.astype(jnp.float32), axis=-1, keepdims=True) * v
    y = (y + bonus.reshape(b, s, RWKV_WIDTH)) * g.astype(jnp.float32)
    return y.astype(f.dtype)

def first_inputs(seed: int = 0) -> dict:
    key = jax.random.key(seed)
    ks = jax.random.split(key, 32)
    L = DEPTH
    nrm = lambda k, shape, scale: jax.random.normal(k, shape, jnp.float32) * scale
    gain = lambda k, shape: 1.0 + 0.05 * jax.random.normal(k, shape, jnp.float32)
    return {
        "x": nrm(ks[0], (BATCH, SEQ, D_MODEL), 1.0),
        "rel_bias": nrm(ks[1], (N_BUCKETS, ATT_HEADS), 0.2),
        "norm_mix_pre": gain(ks[2], (L, D_MODEL)),
        "norm_mix_post": gain(ks[3], (L, D_MODEL)),
        "norm_ffn_pre": gain(ks[4], (L, D_MODEL)),
        "norm_ffn_post": gain(ks[5], (L, D_MODEL)),
        "w_in": nrm(ks[6], (L, D_MODEL, IN_COLS), D_MODEL ** -0.5),
        "b_gate": nrm(ks[7], (L, N_BRANCHES * D_MODEL), 0.02),
        "shift_mu": jax.random.uniform(ks[8], (L, RWKV_COLS), jnp.float32),
        "w0": jax.random.uniform(ks[9], (L, RWKV_WIDTH), jnp.float32, -6.0, 1.0),
        "w_w2": nrm(ks[10], (L, DECAY_LORA, RWKV_WIDTH), 0.1 * DECAY_LORA ** -0.5),
        "a0": nrm(ks[11], (L, RWKV_WIDTH), 0.1),
        "w_a2": nrm(ks[12], (L, ICLR_LORA, RWKV_WIDTH), 0.5 * ICLR_LORA ** -0.5),
        "w_g2": nrm(ks[13], (L, GATE_LORA, RWKV_WIDTH), GATE_LORA ** -0.5),
        "k_k": 0.85 + 0.05 * jax.random.normal(ks[14], (L, RWKV_WIDTH), jnp.float32),
        "k_a": gain(ks[15], (L, RWKV_WIDTH)),
        "r_k": nrm(ks[16], (L, RWKV_HEADS, HEAD_DIM), 0.1),
        "ln_x_w": gain(ks[17], (L, RWKV_WIDTH)),
        "ln_x_b": nrm(ks[18], (L, RWKV_WIDTH), 0.02),
        "w_att_branch": nrm(ks[19], (L, ATT_OUT_WIDTH, D_MODEL), ATT_OUT_WIDTH ** -0.5),
        "w_rwkv_branch": nrm(ks[20], (L, RWKV_WIDTH, D_MODEL), RWKV_WIDTH ** -0.5),
        "w_out": nrm(ks[21], (L, D_MODEL, D_MODEL), D_MODEL ** -0.5),
        "w_ffn1": nrm(ks[22], (L, D_MODEL, D_FF), D_MODEL ** -0.5),
        "w_ffn2": nrm(ks[23], (L, D_FF, D_MODEL), D_FF ** -0.5),
    }

def first_block(x, rel_bias, norm_mix_pre, norm_mix_post, norm_ffn_pre, norm_ffn_post,
              w_in, b_gate, shift_mu, w0, w_w2, a0, w_a2, w_g2, k_k, k_a, r_k,
              ln_x_w, ln_x_b, w_att_branch, w_rwkv_branch, w_out, w_ffn1, w_ffn2):
    b, s, _ = x.shape
    for l in range(DEPTH):
        h = rmsnorm(x, norm_mix_pre[l])
        proj = h @ w_in[l]
        f_att, f_rwkv, f_gate = jnp.split(
            proj, [3 * ATT_WIDTH, 3 * ATT_WIDTH + RWKV_COLS], axis=-1)
        qkv = f_att.reshape(b, s, 3, N_GROUPS, HEADS_PER_GROUP, HEAD_DIM)
        o_att = dilated_window_attention(qkv[:, :, 0], qkv[:, :, 1], qkv[:, :, 2], rel_bias)
        o_rwkv = rwkv7_time_mix(token_shift(f_rwkv, shift_mu[l]), w0[l], w_w2[l], a0[l],
                                w_a2[l], w_g2[l], k_k[l], k_a[l], r_k[l],
                                ln_x_w[l], ln_x_b[l])
        gates = jax.nn.sigmoid(f_gate + b_gate[l]).reshape(b, s, N_BRANCHES, D_MODEL)
        merged = (gates[:, :, 0] * (o_att @ w_att_branch[l])
                  + gates[:, :, 1] * (o_rwkv @ w_rwkv_branch[l]))
        x = x + rmsnorm(merged @ w_out[l], norm_mix_post[l])
        h = rmsnorm(x, norm_ffn_pre[l])
        ff = jnp.square(jax.nn.relu(h @ w_ffn1[l])) @ w_ffn2[l]
        x = x + rmsnorm(ff, norm_ffn_post[l])
    return x


POOL_WIDTH = 512
POOL_WINDOWS = (2, 4, 8, 16)
N_POOL_GROUPS = len(POOL_WINDOWS)
POOL_GROUP = POOL_WIDTH // N_POOL_GROUPS
N_Q_HEADS = 8
N_KV_HEADS = 2
Q_GROUP = N_Q_HEADS // N_KV_HEADS
Q_WIDTH = N_Q_HEADS * HEAD_DIM
KV_WIDTH = N_KV_HEADS * HEAD_DIM
WINDOW = 128
BLOCK = 128
IN_WIDTH = POOL_WIDTH + Q_WIDTH + 2 * KV_WIDTH + N_BRANCHES * D_MODEL
D_FF_2 = ((8 * D_MODEL + 3 * 256 - 1) // (3 * 256)) * 256
EPS = 1e-6


def rms_norm(x, gain):
    xf = x.astype(jnp.float32)
    y = xf * lax.rsqrt(jnp.mean(xf * xf, axis=-1, keepdims=True) + EPS)
    return (y * gain.astype(jnp.float32)).astype(x.dtype)

def alibi_slopes():
    h = jnp.arange(1, N_Q_HEADS + 1, dtype=jnp.float32)
    return jnp.exp2(-8.0 * h / N_Q_HEADS)

def multiscale_pool(z, w_group, scale):
    B, S, _ = z.shape
    zf = z.astype(jnp.float32)
    cs = jnp.pad(jnp.cumsum(zf, axis=1), ((0, 0), (1, 0), (0, 0)))
    t = jnp.arange(S)
    outs = []
    for g, w in enumerate(POOL_WINDOWS):
        sl = slice(g * POOL_GROUP, (g + 1) * POOL_GROUP)
        lo = jnp.clip(t - w // 2, 0, S)
        hi = jnp.clip(t + w // 2, 0, S)
        csg = cs[..., sl]
        count = (hi - lo).astype(jnp.float32)[None, :, None]
        mean = (csg[:, hi] - csg[:, lo]) / count
        outs.append(mean - zf[..., sl])
    d = jnp.stack(outs, axis=2).astype(z.dtype)
    y = jnp.einsum("bsgc,gcd->bsgd", d, w_group).reshape(B, S, POOL_WIDTH)
    return y * scale

def band_blocks(t, nb):
    B = t.shape[0]
    t = jnp.pad(t, ((0, 0), (BLOCK, BLOCK), (0, 0), (0, 0)))
    t = t.reshape(B, nb + 2, BLOCK, N_KV_HEADS, HEAD_DIM)
    return jnp.concatenate([t[:, :-2], t[:, 1:-1], t[:, 2:]], axis=2)

def windowed_gqa(q, k, v, sink):
    B, S, _ = q.shape
    nb = S // BLOCK
    qb = (q * (HEAD_DIM ** -0.5)).reshape(B, nb, BLOCK, N_KV_HEADS, Q_GROUP, HEAD_DIM)
    kb = band_blocks(k.reshape(B, S, N_KV_HEADS, HEAD_DIM), nb)
    vb = band_blocks(v.reshape(B, S, N_KV_HEADS, HEAD_DIM), nb)
    scores = jnp.einsum("bnqhgd,bnkhd->bnhgqk", qb, kb).astype(jnp.float32)
    a = jnp.arange(BLOCK)[:, None]
    c = jnp.arange(3 * BLOCK)[None, :]
    absdist = jnp.abs(a - c + BLOCK)
    kpos = (jnp.arange(nb)[:, None] - 1) * BLOCK + jnp.arange(3 * BLOCK)[None, :]
    kvalid = (kpos >= 0) & (kpos < S)
    mask = (absdist <= WINDOW)[None, :, :] & kvalid[:, None, :]
    slopes = alibi_slopes().reshape(N_KV_HEADS, Q_GROUP)[:, :, None, None]
    scores = scores - slopes * absdist.astype(jnp.float32)
    scores = jnp.where(mask[None, :, None, None, :, :], scores, -jnp.inf)
    sink_l = sink.astype(jnp.float32).reshape(N_KV_HEADS, Q_GROUP)[:, :, None, None]
    m = jnp.maximum(jnp.max(scores, axis=-1, keepdims=True), sink_l)
    p = jnp.exp(scores - m)
    denom = jnp.sum(p, axis=-1, keepdims=True) + jnp.exp(sink_l - m)
    p = (p / denom).astype(v.dtype)
    out = jnp.einsum("bnhgqk,bnkhd->bnqhgd", p, vb)
    return out.reshape(B, S, Q_WIDTH)

def second_inputs(seed: int = 0) -> dict:
    key = jax.random.key(seed)
    ks = jax.random.split(key, 16)
    f32 = jnp.float32

    def dense(k, shape, fan_in):
        return jax.random.normal(k, shape, f32) * (fan_in ** -0.5)

    def gain(k, shape):
        return 1.0 + 0.05 * jax.random.normal(k, shape, f32)

    return {
        "x": jax.random.normal(ks[0], (BATCH, SEQ, D_MODEL), f32),
        "norm_mix": gain(ks[1], (DEPTH, D_MODEL)),
        "w_in": dense(ks[2], (DEPTH, D_MODEL, IN_WIDTH), D_MODEL),
        "w_pool_group": dense(ks[3], (DEPTH, N_POOL_GROUPS, POOL_GROUP, POOL_GROUP), POOL_GROUP),
        "pool_scale": gain(ks[4], (DEPTH, POOL_WIDTH)),
        "sink": 0.5 * jax.random.normal(ks[5], (DEPTH, N_Q_HEADS), f32),
        "w_pool_branch": dense(ks[6], (DEPTH, POOL_WIDTH, D_MODEL), POOL_WIDTH),
        "w_attn_branch": dense(ks[7], (DEPTH, Q_WIDTH, D_MODEL), Q_WIDTH),
        "w_out": dense(ks[8], (DEPTH, D_MODEL, D_MODEL), D_MODEL),
        "norm_ffn": gain(ks[9], (DEPTH, D_MODEL)),
        "w_ffn_gate": dense(ks[10], (DEPTH, D_MODEL, D_FF_2), D_MODEL),
        "w_ffn_up": dense(ks[11], (DEPTH, D_MODEL, D_FF_2), D_MODEL),
        "w_ffn_down": dense(ks[12], (DEPTH, D_FF_2, D_MODEL), D_FF_2),
        "norm_final": gain(ks[13], (D_MODEL,)),
    }

def second_block(x, norm_mix, w_in, w_pool_group, pool_scale, sink, w_pool_branch,
              w_attn_branch, w_out, norm_ffn, w_ffn_gate, w_ffn_up, w_ffn_down, norm_final):
    splits = [POOL_WIDTH,
              POOL_WIDTH + Q_WIDTH,
              POOL_WIDTH + Q_WIDTH + KV_WIDTH,
              POOL_WIDTH + Q_WIDTH + 2 * KV_WIDTH,
              POOL_WIDTH + Q_WIDTH + 2 * KV_WIDTH + D_MODEL]
    h = x
    for l in range(DEPTH):
        u = rms_norm(h, norm_mix[l])
        proj = u @ w_in[l]
        z_pool, q, k, v, g_pool, g_attn = jnp.split(proj, splits, axis=-1)
        y_pool = multiscale_pool(z_pool, w_pool_group[l], pool_scale[l]) @ w_pool_branch[l]
        y_attn = windowed_gqa(q, k, v, sink[l]) @ w_attn_branch[l]
        merged = jax.nn.sigmoid(g_pool) * y_pool + jax.nn.sigmoid(g_attn) * y_attn
        h = h + merged @ w_out[l]
        u = rms_norm(h, norm_ffn[l])
        h = h + (jax.nn.silu(u @ w_ffn_gate[l]) * (u @ w_ffn_up[l])) @ w_ffn_down[l]
    return rms_norm(h, norm_final)


def setup_inputs(seed=0):
    out = dict(first_inputs(seed))
    for name, value in second_inputs(seed + 1).items():
        if name != "x":
            out[name + "_2"] = value
    return out


def reference(
    x, rel_bias, norm_mix_pre, norm_mix_post, norm_ffn_pre, norm_ffn_post, w_in, b_gate,
    shift_mu, w0, w_w2, a0, w_a2, w_g2, k_k, k_a, r_k, ln_x_w, ln_x_b, w_att_branch,
    w_rwkv_branch, w_out, w_ffn1, w_ffn2, norm_mix_2, w_in_2, w_pool_group_2, pool_scale_2,
    sink_2, w_pool_branch_2, w_attn_branch_2, w_out_2, norm_ffn_2, w_ffn_gate_2, w_ffn_up_2,
    w_ffn_down_2, norm_final_2,
):
    x = first_block(
        x, rel_bias, norm_mix_pre, norm_mix_post, norm_ffn_pre, norm_ffn_post, w_in, b_gate,
        shift_mu, w0, w_w2, a0, w_a2, w_g2, k_k, k_a, r_k, ln_x_w, ln_x_b, w_att_branch,
        w_rwkv_branch, w_out, w_ffn1, w_ffn2,
    )
    return second_block(
        x, norm_mix_2, w_in_2, w_pool_group_2, pool_scale_2, sink_2, w_pool_branch_2,
        w_attn_branch_2, w_out_2, norm_ffn_2, w_ffn_gate_2, w_ffn_up_2, w_ffn_down_2,
        norm_final_2,
    )


_drawn_inputs = setup_inputs


def setup_inputs(seed=0):
    import zlib

    import numpy as np

    out = dict(_drawn_inputs(seed))
    spreads = {}
    factors = {'b_gate': 8.0,
     'w_w2': 8.0,
     'ln_x_b': 3.846,
     'norm_mix_2': 3.563,
     'pool_scale_2': 4.368,
     'sink_2': 64.0,
     'norm_ffn_2': 8.0}
    for name, (base, spread) in spreads.items():
        noise = np.random.default_rng([zlib.crc32(name.encode()), seed]).standard_normal(out[name].shape)
        drawn = base * np.exp(spread * noise) if base else spread * noise
        out[name] = __import__('jax').numpy.asarray(drawn.astype(out[name].dtype))
    for name, factor in factors.items():
        out[name] = (out[name] * factor).astype(out[name].dtype)
    return out
```

```python
import math
from contextlib import ExitStack

import numpy as np

import concourse.bass as bass
from concourse import mybir

F32 = mybir.dt.float32
F32R = mybir.dt.float32r
I32 = mybir.dt.int32
ACT = mybir.ActivationFunctionType
ALU = mybir.AluOpType
AX = mybir.AxisListType

P = 128
T = 512
NT = T // P
D = 1024
KT = D // P
HD = 64
UNIT = 2048
NEG = -1e30
KAPPA = math.exp(-0.5)
EPS = 1e-6
LN_EPS = 64e-5
L2_EPS2 = 1e-24

ATT_W = 768
N_GROUPS = 3
DILATIONS = (1, 4, 16)
KEYS = 128
N_BUCKETS = 32
MAX_DIST = KEYS * DILATIONS[-1]
RW = 1024
PAIRS = 8
FF1_GROUPS = 16
D_FF2 = 2816
FF2_GROUPS = D_FF2 // 256
POOL_W = 512
Q_HEADS2 = 8
LEVELS = (2, 4, 8, 16, 32, 64, 128)
DVE_STEPS = 52

STAGES = [("qk", 6), ("v", 3), ("lora", 1), ("rwkv", 16), ("gate0", 4), ("attb", 1), ("rwkvb", 4),
          ("wout", 4), ("ffn", 2 * FF1_GROUPS), ("pool", 2), ("q2", 2), ("kv2", 1), ("group", 1),
          ("gatep", 4), ("gatea", 4), ("poolb", 2), ("attnb", 2), ("wout2", 4), ("ffn2", 3 * FF2_GROUPS)]
USES = dict(qk=6, v=3, lora=1, gate0=4, attb=4, rwkv=16, rwkvb=4, wout=4, ffn=FF1_GROUPS, pool=2, q2=2,
            kv2=1, gatep=4, gatea=4, group=2, poolb=4, attnb=4, wout2=4, ffn2=2 * FF2_GROUPS)
UNIT0, USE0 = {}, {}
_n = _d = 0
for _name, _count in STAGES:
    UNIT0[_name], USE0[_name] = _n, _d
    _n += _count
    _d += USES[_name]
N_UNITS = _n

PCOLS = [("mu", 26), ("w0", 8), ("a0", 8), ("k_k", 8), ("k_a", 8), ("r_k", 8), ("ln_w", 8), ("ln_b", 8),
         ("b_gate", 16), ("mix_pre", 8), ("ffn_pre", 8), ("mix2", 8), ("ffn2", 8), ("pool_scale", 4)]
PC = {}
_c = 0
for _name, _count in PCOLS:
    PC[_name] = _c
    _c += _count
N_PCOLS = _c

CCOLS = [("ident", P), ("ones_head", P), ("ones", P), ("strict_incl", 2 * P), ("levels", len(LEVELS) * P),
         ("absdist", 3 * P), ("eps", 1), ("ln_eps", 1)]
CC = {}
_c = 0
for _name, _count in CCOLS:
    CC[_name] = _c
    _c += _count
N_CCOLS = _c
TOE_LEN = 640


def constants():
    p = np.arange(P)[:, None]
    c = np.arange(P)[None, :]
    tab = np.zeros((P, N_CCOLS), np.float32)

    def put(name, a):
        tab[:, CC[name]:CC[name] + a.shape[1]] = a

    put("ident", (p == c).astype(np.float32))
    put("ones_head", (p // HD == c // HD).astype(np.float32))
    put("ones", np.ones((P, P), np.float32))
    put("strict_incl", np.concatenate([(p <= c), (p < c)], 1).astype(np.float32))
    put("levels", np.concatenate([((p // b == c // b) & (p % b < b // 2) & (c % b >= b // 2))
                                  for b in LEVELS], 1).astype(np.float32))
    x = np.arange(3 * P)[None, :]
    dist = np.abs(p - (x - P))
    put("absdist", np.where(dist <= P, dist, 1e30).astype(np.float32))
    put("eps", np.full((P, 1), EPS, np.float32))
    put("ln_eps", np.full((P, 1), LN_EPS, np.float32))
    return tab


def bucket_table():
    out = np.zeros((N_BUCKETS + 1, N_GROUPS * TOE_LEN), np.float32)
    exact = N_BUCKETS // 2
    for g, d in enumerate(DILATIONS):
        for v in range(TOE_LEN):
            dist = T - 1 - v
            row = N_BUCKETS
            if dist >= 0 and dist % d == 0 and dist // d <= KEYS:
                if dist < exact:
                    row = dist
                else:
                    big = exact + int(np.float32(np.log(np.float32(dist) / np.float32(exact)))
                                      / np.float32(math.log(MAX_DIST / exact)) * np.float32(N_BUCKETS - exact))
                    row = min(big, N_BUCKETS - 1)
            out[row, g * TOE_LEN + v] = 1.0
    return out


def inv_counts():
    t = np.arange(T)
    rows = []
    for w in (2, 4, 8, 16):
        n = np.clip(t + w // 2, 0, T) - np.clip(t - w // 2, 0, T)
        rows.append(1.0 / n.astype(np.float32))
    return np.stack(rows).astype(np.float32)



def build(nc, x, wpack, lora_wa, lora_g, params, rel_bias, post_gains, sink, ctab, btab, icount, out):
    toe_dram = nc.dram_tensor("bias_rows_dram", (4, N_GROUPS, TOE_LEN), F32, kind="Internal").ap()
    SKEW = P * (TOE_LEN + 1)
    toe_skew = nc.dram_tensor("bias_skewed_dram", (12, SKEW), F32, kind="Internal").ap()

    with ExitStack() as ctx:
        top = [nc.sbuf_base + (-nc.sbuf_base) % 64]

        def place(name, shape, dt=F32, at=None):
            size = 4 * int(np.prod(shape[1:]))
            if at is None:
                at = top[0]
                top[0] += size + (-size) % 64
            return nc.alloc_sbuf_tensor_at(name, shape, dt, offset=at), at + size + (-size) % 64

        def fixed(name, shape, dt=F32):
            return place(name, shape, dt)[0]

        class Region:

            def __init__(self, at):
                self.at = at

            def __call__(self, name, shape, dt=F32):
                t, self.at = place(name, shape, dt, self.at)
                assert self.at <= nc.sbuf_usable_end, (name, self.at - nc.sbuf_usable_end)
                return t

        def sem(name):
            return ctx.enter_context(nc.semaphore(name))

        Xr = fixed("x_res", [P, NT, D])
        x_at = top[0] - 4 * NT * D
        Y = fixed("y_tok", [P, NT, D])
        y_at = top[0] - 4 * NT * D
        HTh = fixed("ht_hi", [P, KT, T], F32R)
        HTl = fixed("ht_lo", [P, KT, T], F32R)
        raw = fixed("w_raw", [P, 2, UNIT])
        Wh = fixed("w_hi", [P, 2, UNIT], F32R)
        Wl = fixed("w_lo", [P, 2, UNIT], F32R)
        C = fixed("consts", [P, N_CCOLS])
        PR = fixed("params_sb", [P, N_PCOLS])
        stat = fixed("stat", [P, 64])
        OAT = fixed("att_out", [P, 2, T])
        FWA = fixed("lora_in", [P, 2, T])
        base = top[0]

        r = Region(base)
        QK = r("qk_t", [P, 12, T])
        V1 = r("v_tok", [P, NT, ATT_W])
        TOE = r("toe", [P, 12, T])
        LG1 = r("logits1", [P, 2, 1280])
        PT1 = r("probs_t1", [P, 10, P])
        r = Region(base)
        RB = r("rel_bias_sb", [N_BUCKETS + 1, 12])
        BT = r("buckets_sb", [N_BUCKETS + 1, N_GROUPS * TOE_LEN])
        RROW = r("bias_rows", [4, N_GROUPS, TOE_LEN])
        r = Region(base + 4 * (12 * T + NT * ATT_W + 12 * T))
        LRAW = r("lora_raw", [P, 2, T + 1])
        LTMP = r("lora_tmp", [P, 2, T])
        ORW = place("rwkv_out", [P, PAIRS, T], at=x_at)[0]
        G1 = place("gate1", [P, KT, T], at=y_at)[0]
        r = Region(base)
        LWA = r("lora_wa_sb", [P, 2 * P])
        LGW = r("lora_g_sb", [P, 2 * P])
        RAW = r("rkv", [P, 3, 2, T + 1])
        SZ = r("sig_w", [P, T])
        Ab = r("iclr", [P, T])
        Gb = r("rwkv_gate", [P, T])
        CS = r("cum_decay", [P, T])
        KK = r("kk", [P, T])
        E = r("work_e", [P, T])
        T1 = r("work_t", [P, T])
        X2 = r("work_x", [P, T])
        RA = r("ra", [P, NT, 2, P])
        KB = r("kb", [P, 2, T])
        TV = r("v_chunk", [P, NT, P])
        TK = r("k_chunk", [P, NT, P])
        TB = r("b_chunk", [P, NT, P])
        GM = [r(f"gram{h}", [P, NT, 4, P]) for h in range(2)]
        Mb = [r(f"level{h}", [P, NT, P]) for h in range(2)]
        Xb = [r(f"xinv{h}", [P, NT, P]) for h in range(2)]
        Tb = [r(f"tinv{h}", [P, NT, P]) for h in range(2)]
        TT = [r(f"tinv_t{h}", [P, NT, P]) for h in range(2)]
        S = r("state", [P, HD])
        RH = r("rhs_sb", [P, P])
        SA = r("sa_sb", [P, P])
        LM = r("mid_decay", [P, 2, NT])
        K16 = 4 * KT * T
        MG = place("merged", [P, KT, T], at=base)[0]
        ORh = place("rwkv_hi", [P, KT, T], F32R, at=base + K16)[0]
        ORl = place("rwkv_lo", [P, KT, T], F32R, at=base + 2 * K16)[0]
        OAh = place("att_hi", [P, 2, T], F32R, at=base + 3 * K16)[0]
        OAl = place("att_lo", [P, 2, T], F32R, at=base + 3 * K16 + K16 // 4)[0]
        GN = place("gains", [P, D], at=base + 4 * K16)[0]
        JUNK = place("squares", [P, D], at=base + 4 * K16 + K16 // 4)[0]
        r = Region(base)
        HIh = r("hid_hi", [P, 2, 2, T], F32R)
        HIl = r("hid_lo", [P, 2, 2, T], F32R)
        HR = r("hid_raw", [P, 2, T])
        HR2 = r("hid_sq", [P, 2, T])
        r = Region(base)
        Zp = r("pool_z", [P, 4, T + 32])
        Q2 = r("q2_t", [P, 4, T])
        KD = r("k2_t", [P, 2, T])
        V2 = r("v2_tok", [P, NT, P])
        pd_at = r.at
        PDh = r("pool_hi", [P, 4, T], F32R)
        PDl = r("pool_lo", [P, 4, T], F32R)
        YPh = r("yp_hi", [P, 4, T], F32R)
        YPl = r("yp_lo", [P, 4, T], F32R)
        O2 = r("att2_out", [P, 4, T])
        LG2 = r("logits2", [P, 2, 3 * P])
        PT2 = r("probs_t2", [P, 3, P])
        SNK = r("sink_sb", [P, Q_HEADS2])
        PW = r("pool_tmp", [P, 2, T + 32])
        IC = place("icount_sb", [P, 4, T], at=y_at)[0]
        MG2 = place("merged2", [P, KT, T], at=base)[0]
        G2 = place("gate_att2", [P, KT, T], at=pd_at)[0]
        O2h = place("att2_hi", [P, 4, T], F32R, at=y_at)[0]
        O2l = place("att2_lo", [P, 4, T], F32R, at=y_at + K16 // 2)[0]
        ps = ctx.enter_context(nc.psum_tensor("ps", [P, 8, 512], F32))

        ident = C[:, CC["ident"]:CC["ident"] + P]
        ones_head = C[:, CC["ones_head"]:CC["ones_head"] + P]
        ones = C[:, CC["ones"]:CC["ones"] + P]

        consts_in, params_in, x_in, bias_in = (sem(n) for n in ("consts_in", "params_in", "x_in", "bias_in"))
        unit_in = [sem("unit_in_even"), sem("unit_in_odd")]
        hi_ready, lo_ready = sem("hi_ready"), sem("lo_ready")
        pair_full = sem("pair_full")
        half_done = sem("half_done")
        row_full = sem("row_full")
        row_taken = sem("row_taken")
        pair_taken = [sem("pair_taken_even"), sem("pair_taken_odd")]
        dve_order, act_order = sem("dve_order"), sem("act_order")
        rms_ready, xn_ready, ht_full, ht_hi, ht_lo = (
            sem(n) for n in ("rms_ready", "xn_ready", "ht_full", "ht_hi", "ht_lo"))
        rb_ready, rows_full, rows_ready, toe_stored, toe_skewed, toe_in = (
            sem(n) for n in ("rb_ready", "rows_full", "rows_ready", "toe_stored", "toe_skewed", "toe_in"))
        lora_pad, lora_raw_in, lora_shifted, lora_act = (
            sem(n) for n in ("lora_pad", "lora_raw_in", "lora_shifted", "lora_act"))
        lg_full, lg_read, nmx_ready, exp_ready, prob_ready, pt_full, pt_taken, pv_full, o_taken = (
            sem(n) for n in ("lg_full", "lg_read", "nmx_ready", "exp_ready", "prob_ready", "pt_full",
                             "pt_taken", "pv_full", "o_taken"))
        sink_in, ic_in, kd_in, x_back, gain_in, out_done = (
            sem(n) for n in ("sink_in", "ic_in", "kd_in", "x_back", "gain_in", "out_done"))
        gate_ready, merged_hi, merged_lo, split_hi, split_lo, x_ready, yrms_ready = (
            sem(n) for n in ("gate_ready", "merged_hi", "merged_lo", "split_hi", "split_lo", "x_ready", "yrms_ready"))
        hid_raw, hid_sq, hid_hi, hid_lo = (sem(n) for n in ("hid_raw", "hid_sq", "hid_hi", "hid_lo"))
        y_ready, z_ready, pd_ready, kraw_ready = (sem(n) for n in ("y_ready", "z_ready", "pd_ready", "kraw_ready"))
        lora_w_in = sem("lora_w_in")
        pair_open = sem("pair_open")
        rs = {n: sem(n) for n in ("z_full", "sig_ready", "z_read", "sq_ready", "ss_full", "nrm_ready", "sqrt_ready",
                                  "rk_ready", "bonus_full", "csm_ready", "exps_ready", "rakb_ready",
                                  "tok_full", "tok_ready", "gram_full", "gram_taken", "m_ready", "x_full",
                                  "x1_ready", "tt_full", "t_ready", "t2_ready", "s_ready", "rhs_full", "rhs_ready",
                                  "sa_full", "sa_ready", "s_full", "y_full", "yraw_ready", "mu_full",
                                  "ysq_ready", "var_full", "std_ready", "tt_last")}
        dve_rwkv = sem("dve_rwkv_order")

        class Order:

            def __init__(self, eng, s, base=0):
                self.eng, self.sem, self.base, self.n = eng, s, base, 0

            def __call__(self, ins):
                ins.then_inc(self.sem, 1)
                self.n += 1
                self.eng.wait_ge(self.sem, self.n + self.base)

        def f32(ap):
            return ap.bitcast(F32)

        def bank(b, n=512):
            return ps[:, b, 0:n]

        def pcol(name, k=0):
            c = PC[name] + k
            return PR[:, c:c + 1]

        def pcol_dyn(name, k):
            return PR[:, bass.ds(k + PC[name], 1)]

        read_by = {}
        for name, count in STAGES:
            n0, d0 = UNIT0[name], USE0[name]
            for u in range(count):
                if name in ("wout", "wout2"):
                    k = 2 * (name == "wout2") + u // 2 + 1
                    read_by[n0 + u] = (half_done, k) if u % 2 == 0 else (pair_full, d0 + u + 1)
                elif name not in ("ffn", "ffn2"):
                    read_by[n0 + u] = (pair_full, d0 + (u + 1) * (USES[name] // count))
        for name, groups, ups, rows0 in (("ffn", FF1_GROUPS, 1, 0), ("ffn2", FF2_GROUPS, 2, NT * FF1_GROUPS)):
            n, d = UNIT0[name], USE0[name]
            for g in range(groups + 1):
                if g < groups:
                    for _ in range(ups):
                        d += 1
                        read_by[n] = (pair_full, d)
                        n += 1
                if g > 0:
                    read_by[n] = (row_full, rows0 + NT * g)
                    n += 1

        items1 = []
        for hh in range(4):
            for qt in range(NT):
                segs, vals, off = [], [], 0
                for g in range(N_GROUPS):
                    nb = min(2, qt + 1) if g == 0 else qt + 1
                    h = g * 4 + hh
                    rows = slice(HD * (h % 2), HD * (h % 2) + HD)
                    k0 = (qt + 1 - nb) * P
                    segs.append(dict(bank=4 + g, n=nb * P, off=off,
                                     q=QK[rows, h // 2, qt * P:(qt + 1) * P],
                                     k=QK[rows, 6 + h // 2, k0:(qt + 1) * P],
                                     bias=TOE[:, hh * 3 + g, T - nb * P:T]))
                    off += nb * P
                    vals += [V1[:, kb, h * HD:(h + 1) * HD] for kb in range(qt + 1 - nb, qt + 1)]
                items1.append(dict(segs=segs, vals=vals, n=off, rows=slice(HD * (hh % 2), HD * (hh % 2) + HD),
                                   out=OAT[HD * (hh % 2):HD * (hh % 2) + HD, hh // 2, qt * P:(qt + 1) * P]))
        items2 = []
        for h in range(Q_HEADS2):
            for qt in range(NT):
                lo, hi = max(0, qt - 1), min(NT, qt + 2)
                rows = slice(HD * (h % 2), HD * (h % 2) + HD)
                kv = h // 4
                x0 = (lo - (qt - 1)) * P
                n = (hi - lo) * P
                items2.append(dict(
                    segs=[dict(bank=4 + len(items2) % 3, n=n, off=0, q=Q2[rows, h // 2, qt * P:(qt + 1) * P],
                               k=KD[rows, kv, lo * P:hi * P],
                               slope=-(2.0 ** -(h + 1)),
                               bias=C[:, CC["absdist"] + x0:CC["absdist"] + x0 + n])],
                    vals=[V2[:, kb, kv * HD:(kv + 1) * HD] for kb in range(lo, hi)], n=n, sink=h, rows=rows,
                    out=O2[rows, h // 2, qt * P:(qt + 1) * P]))
        att = [dict(items=items1, LG=LG1, PT=PT1, first=0), dict(items=items2, LG=LG2, PT=PT2, first=len(items1))]
        chunk = 0
        for a in att:
            for it in a["items"]:
                nv = len(it["vals"])
                it["chunks"] = [(c, min(4, nv - c)) for c in range(0, nv, 4)]
                it["chunk0"] = chunk
                chunk += len(it["chunks"])
                it["chunk1"] = chunk

        block = ctx.enter_context(nc.Block())

        @block.sync
        def _(sp):
            def load(n, slot):
                sp.dma_start(raw[:, slot, :], wpack[bass.ds(n, 1)].rearrange("a p f -> p (a f)")
                             if not isinstance(n, int) else wpack[n]).then_inc(unit_in[slot], 16)

            sp.dma_start(Xr[:], x.rearrange("(t p) d -> p t d", p=P)).then_inc(x_in, 16)
            sp.dma_start(C[:], ctab).then_inc(consts_in, 16)
            sp.dma_start(PR[:], params).then_inc(params_in, 16)
            sp.dma_start(RB[0:N_BUCKETS, :], rel_bias).then_inc(bias_in, 16)
            sp.dma_start(BT[:], btab).then_inc(bias_in, 16)
            load(0, 0)
            load(1, 1)
            with sp.Fori(1, N_UNITS // 2) as i:
                for slot in range(2):
                    sp.wait_ge(lo_ready, i * 2 + (slot - 1))
                    load(i * 2 + slot, slot)

        @block.gpsimd
        def _(pool):
            for n in range(N_UNITS):
                slot = n % 2
                pool.wait_ge(unit_in[slot], 16 * (n // 2 + 1))
                if n >= 2:
                    pool.wait_ge(*read_by[n - 2])
                nc.gpsimd.tensor_copy(Wh[:, slot, :], raw[:, slot, :]).then_inc(hi_ready, 1)
                pool.wait_ge(hi_ready, n + 1)
                nc.gpsimd.tensor_tensor(Wl[:, slot, :], raw[:, slot, :], f32(Wh[:, slot, :]),
                                        ALU.subtract).then_inc(lo_ready, 1)

        @block.tensor
        def _(pe):
            mm = nc.tensor.matmul

            def mm3(dst, wh, wl, ah, al, first, last):
                mm(dst, wh, ah, start=first, stop=False)
                mm(dst, wh, al, start=False, stop=False)
                return mm(dst, wl, ah, start=False, stop=last)

            def wait_pair(name, i, per, j, d):
                par = d % 2
                if isinstance(i, int):
                    if d + per * i >= 2:
                        pe.wait_ge(pair_taken[par], (d + per * i) // 2)
                else:
                    pe.wait_ge(pair_taken[par], i * (per // 2) + d // 2)

            def unit_cm(name, i, per, j, act=None, kts=KT, dper=None, dj=None):
                n, dper = UNIT0[name] + j, per if dper is None else dper
                d = USE0[name] + (j if dj is None else dj)
                ah, al = act or (HTh, HTl)
                cols = UNIT // kts
                slot = n % 2
                wh = Wh[:, slot, :].rearrange("p (k c) -> p k c", k=kts)
                wl = Wl[:, slot, :].rearrange("p (k c) -> p k c", k=kts)
                pe.wait_ge(lo_ready, i * per + (n + 1))
                for use in range(cols // 256):
                    wait_pair(name, i, dper, 0, d + use)
                    for c in range(2):
                        cc = use * 256 + c * P
                        for k in range(kts):
                            last = mm3(bank(2 * ((d + use) % 2) + c), wh[:, k, cc:cc + P], wl[:, k, cc:cc + P],
                                       ah[:, k, :], al[:, k, :], k == 0, k == kts - 1)
                    last.then_inc(pair_full, 1)

            def rows_of(slot, kts, k, c0, n):
                a = k * (UNIT // kts) + c0
                return Wh[:, slot, a:a + n], Wl[:, slot, a:a + n]

            def transposes(k):
                pe.wait_ge(xn_ready, NT * (k + 1))
                for kt in range(KT):
                    if k or kt >= 4:
                        pe.wait_ge(ht_lo, KT * k + kt - 3)
                    for tt in range(NT):
                        last = nc.tensor.transpose(ps[:, 4 + kt % 4, tt * P:(tt + 1) * P],
                                                   Y[:, tt, kt * P:(kt + 1) * P], ident)
                    last.then_inc(ht_full, 1)

            def attention(a):
                items, first, LG, PT = a["items"], a["first"], a["LG"], a["PT"]

                def logits(i):
                    if first + i:
                        pe.wait_ge(lg_read, first + i)
                    for s in items[i]["segs"]:
                        last = mm(bank(s["bank"], s["n"]), s["q"], s["k"], start=True, stop=True)
                    last.then_inc(lg_full, 1)

                logits(0)
                for i, it in enumerate(items):
                    if i + 1 < len(items):
                        logits(i + 1)
                    pe.wait_ge(prob_ready, first + i + 1)
                    for c, (v0, nv) in enumerate(it["chunks"]):
                        g = it["chunk0"] + c
                        if g >= 2:
                            pe.wait_ge(pt_taken, g - 1)
                        for j in range(nv):
                            last = nc.tensor.transpose(ps[:, 7 - 4 * (g % 2), j * P:(j + 1) * P],
                                                       LG[:, i % 2, (v0 + j) * P:(v0 + j + 1) * P], ident)
                        last.then_inc(pt_full, 1)
                    pe.wait_ge(pt_taken, it["chunk1"])
                    if first + i:
                        pe.wait_ge(o_taken, first + i)
                    for j, v in enumerate(it["vals"]):
                        last = mm(ps[it["rows"], 2, 0:P], v, PT[:, j, :], start=j == 0, stop=j == len(it["vals"]) - 1)
                    last.then_inc(pv_full, 1)

            def tok_major_out(name, k):
                for cb in range(2):
                    d = USE0[name] + 2 * cb
                    for half in range(2):
                        n = UNIT0[name] + 2 * cb + half
                        pe.wait_ge(lo_ready, n + 1)
                        for tt in range(NT):
                            use = d + tt // 2
                            if half == 0 and tt % 2 == 0:
                                wait_pair(name, 0, 0, 0, use)
                            for kk in range(4):
                                wh, wl = rows_of(n % 2, 4, kk, 0, 512)
                                kt = 4 * half + kk
                                tok = slice(tt * P, (tt + 1) * P)
                                last = mm3(bank(2 * (use % 2) + tt % 2), HTh[:, kt, tok], HTl[:, kt, tok],
                                           wh, wl, kt == 0, kt == KT - 1)
                            if half == 1 and tt % 2 == 1:
                                last.then_inc(pair_full, 1)
                        if half == 0:
                            last.then_inc(half_done, 1)

            def down(n_static, n_expr, g_static, rows_expr, hid_expr):
                pe.wait_ge(lo_ready, n_expr)
                pe.wait_ge(hid_lo, hid_expr)
                for tt in range(NT):
                    b = 4 + 2 * (tt % 2)
                    if rows_expr is not None or tt >= 2:
                        pe.wait_ge(row_taken, (rows_expr if rows_expr is not None else 0) + (tt - 1))
                    for k in range(2):
                        tok = slice(tt * P, (tt + 1) * P)
                        for c in range(2):
                            wh, wl = rows_of(n_static % 2, 2, k, c * 512, 512)
                            last = mm3(bank(b + c), HIh[:, g_static % 2, k, tok], HIl[:, g_static % 2, k, tok],
                                       wh, wl, k == 0, k == 1)
                    last.then_inc(row_full, 1)

            pe.wait_ge(bias_in, 32)
            pe.wait_ge(rb_ready, 1)
            for g in range(N_GROUPS):
                mm(ps[0:4, 4 + g, 0:T], RB[:, 4 * g:4 * g + 4], BT[:, g * TOE_LEN:g * TOE_LEN + T],
                   start=True, stop=True)
                last = mm(ps[0:4, 7, g * P:(g + 1) * P], RB[:, 4 * g:4 * g + 4],
                          BT[:, g * TOE_LEN + T:(g + 1) * TOE_LEN], start=True, stop=True)
            last.then_inc(rows_full, 1)

            pe.wait_ge(consts_in, 16)
            pe.wait_ge(rows_ready, 1)
            transposes(0)
            pe.wait_ge(ht_lo, KT)
            unit_cm("qk", 0, 2, 0)
            unit_cm("qk", 0, 2, 1)
            with pe.Fori(1, 3) as i:
                unit_cm("qk", i, 2, 0)
                unit_cm("qk", i, 2, 1)
            for u in range(3):
                n, d = UNIT0["v"] + u, USE0["v"] + u
                pe.wait_ge(lo_ready, n + 1)
                wait_pair("v", 0, 0, 0, d)
                for tt in range(NT):
                    for k in range(KT):
                        wh, wl = rows_of(n % 2, KT, k, 0, 256)
                        tok = slice(tt * P, (tt + 1) * P)
                        c0 = 256 * (tt % 2)
                        last = mm3(ps[:, 2 * (d % 2) + tt // 2, c0:c0 + 256], HTh[:, k, tok], HTl[:, k, tok],
                                   wh, wl, k == 0, k == KT - 1)
                last.then_inc(pair_full, 1)
            unit_cm("lora", 0, 0, 0)
            for par in range(2):
                pe.wait_ge(pair_taken[par], (USE0["rwkv"] + 1 - par) // 2)
            pe.wait_ge(toe_in, 16)
            attention(att[0])
            pe.wait_ge(o_taken, len(items1))

            with pe.Fori(0, 4) as q:
                for j in range(4):
                    unit_cm("rwkv", q, 4, j)
                for pp in range(2):
                    def w(name, m, k, pp=pp):
                        pe.wait_ge(rs[name], q * (2 * m) + (m * pp + k))

                    def inc(ins, name):
                        ins.then_inc(rs[name], 1)

                    pe.wait_ge(lora_w_in, q * 32 + 32)
                    pe.wait_ge(lora_act, 3)
                    pe.wait_ge(pair_open, q * 2 + (pp + 1))
                    cols = slice(pp * P, (pp + 1) * P)
                    mm(bank(4), LWA[0:HD, cols], FWA[0:HD, 0, :], start=True, stop=True)
                    mm(bank(5), LWA[HD:P, cols], FWA[HD:P, 0, :], start=True, stop=True)
                    inc(mm(bank(6), LGW[:, cols], FWA[:, 1, :], start=True, stop=True), "z_full")
                    w("sq_ready", 1, 1)
                    inc(mm(bank(7), ones_head, X2[:], start=True, stop=True), "ss_full")
                    w("rk_ready", 1, 1)
                    w("z_read", 1, 1)
                    inc(mm(bank(4), ones_head, T1[:], start=True, stop=True), "bonus_full")
                    w("rakb_ready", 1, 1)
                    for b, src in ((5, RAW[:, 2, pp, 1:T + 1]), (6, KB[:, 0, :]), (7, KB[:, 1, :])):
                        for t in range(NT):
                            last = nc.tensor.transpose(ps[:, b, t * P:(t + 1) * P], src[:, t * P:(t + 1) * P], ident)
                        inc(last, "tok_full")
                    w("tok_ready", 3, 3)
                    for t in range(NT):
                        if t >= 2:
                            w("gram_taken", NT, t - 1)
                        for h in range(2):
                            rows = slice(HD * h, HD * h + HD)
                            b = 4 + 2 * (t % 2) + h
                            ra = RA[rows, t, :, :].rearrange("p a b -> p (a b)")
                            mm(ps[:, b, 0:256], KB[rows, 0, t * P:(t + 1) * P], ra, start=True, stop=True)
                            last = mm(ps[:, b, 256:512], KB[rows, 1, t * P:(t + 1) * P], ra, start=True, stop=True)
                        inc(last, "gram_full")
                    nl = len(LEVELS)
                    for lv in range(nl):
                        for h in range(2):
                            w("m_ready", 2 * nl, 2 * lv + h + 1)
                            if lv >= 1:
                                w("t2_ready", 2, h + 1) if lv == 1 else w("t_ready", 2 * (nl - 2), 2 * (lv - 2) + h + 1)
                            for t in range(NT):
                                last = mm(ps[:, 4 + h, t * P:(t + 1) * P], Mb[h][:, t, :],
                                          Tb[h][:, t, :] if lv else ident, start=True, stop=True)
                            inc(last, "x_full")
                        if lv == 0:
                            continue
                        for h in range(2):
                            w("x1_ready", 2 * (nl - 1), 2 * (lv - 1) + h + 1)
                            if lv < nl - 1:
                                for t in range(NT):
                                    mm(ps[:, 4 + h, t * P:(t + 1) * P], TT[h][:, t, :], Xb[h][:, t, :],
                                       start=True, stop=True)
                            for t in range(NT):
                                last = mm(ps[:, 6 + h, t * P:(t + 1) * P], Xb[h][:, t, :], TT[h][:, t, :],
                                          start=True, stop=True)
                            inc(last, "tt_full")
                    w("t_ready", 2 * (nl - 2), 2 * (nl - 2))
                    w("s_ready", NT, 1)
                    w("tt_last", 2, 2)
                    for t in range(NT):
                        tok = slice(t * P, (t + 1) * P)
                        if t:
                            w("s_ready", NT, t + 1)
                        for h in range(2):
                            rows, hc = slice(HD * h, HD * h + HD), slice(HD * h, HD * h + HD)
                            mm(bank(4 + h, HD), RA[rows, t, 1, :], S[rows, :], start=True, stop=False)
                            last = mm(bank(4 + h, HD), GM[h][:, t, 1, :], TV[:, t, hc], start=False, stop=True)
                        inc(last, "rhs_full")
                        w("rhs_ready", NT, t + 1)
                        for h in range(2):
                            hc = slice(HD * h, HD * h + HD)
                            last = mm(ps[:, 4, P + HD * h:P + HD * h + HD], TT[h][:, t, :], RH[:, hc], start=True, stop=True)
                        inc(last, "sa_full")
                        for h in range(2):
                            rows, hc = slice(HD * h, HD * h + HD), slice(HD * h, HD * h + HD)
                            mm(ps[rows, 6, tok], S[rows, :], RA[rows, t, 0, :], start=True, stop=False)
                            mm(ps[rows, 6, tok], TV[:, t, hc], GM[h][:, t, 0, :], start=False, stop=False)
                        w("sa_ready", NT, t + 1)
                        if t < NT - 1:
                            for h in range(2):
                                rows, hc = slice(HD * h, HD * h + HD), slice(HD * h, HD * h + HD)
                                mm(ps[rows, 5, P:P + HD], TB[:, t, hc], SA[:, hc], start=True, stop=False)
                                last = mm(ps[rows, 5, P:P + HD], TK[:, t, hc], TV[:, t, hc], start=False, stop=True)
                            inc(last, "s_full")
                        for h in range(2):
                            rows, hc = slice(HD * h, HD * h + HD), slice(HD * h, HD * h + HD)
                            last = mm(ps[rows, 6, tok], SA[:, hc], GM[h][:, t, 2, :], start=False, stop=True)
                    inc(last, "y_full")
                    w("yraw_ready", 1, 1)
                    inc(mm(bank(4), ones_head, E[:], start=True, stop=True), "mu_full")
                    w("ysq_ready", 1, 1)
                    inc(mm(bank(5), ones_head, X2[:], start=True, stop=True), "var_full")

            unit_cm("gate0", 0, 2, 0)
            unit_cm("gate0", 0, 2, 1)
            unit_cm("gate0", 1, 2, 0)
            unit_cm("gate0", 1, 2, 1)
            pe.wait_ge(split_lo, 1)
            unit_cm("attb", 0, 0, 0, act=(OAh, OAl), kts=2)
            pe.wait_ge(split_lo, 2)
            for i in range(2):
                unit_cm("rwkvb", i, 2, 0, act=(ORh, ORl))
                unit_cm("rwkvb", i, 2, 1, act=(ORh, ORl))
            pe.wait_ge(merged_lo, 1)
            tok_major_out("wout", 0)
            transposes(1)
            pe.wait_ge(ht_lo, 2 * KT)
            n0 = UNIT0["ffn"]
            unit_cm("ffn", 0, 0, 0)

            def up1(i, per, j, k):
                n = n0 + k
                pe.wait_ge(lo_ready, i * 4 + (n + 1))
                d = USE0["ffn"] + j
                wait_pair("ffn", i, 2, 0, d)
                for c in range(2):
                    for kt in range(KT):
                        wh, wl = rows_of(n % 2, KT, kt, c * P, P)
                        last = mm3(bank(2 * (d % 2) + c), wh, wl, HTh[:, kt, :], HTl[:, kt, :], kt == 0, kt == KT - 1)
                last.then_inc(pair_full, 1)

            def ffn1_step(i, rows):
                up1(i, 2, 1, 1)
                down(n0 + 2, i * 4 + (n0 + 3), 0, rows(0), i * 2 + 1)
                up1(i, 2, 2, 3)
                down(n0 + 4, i * 4 + (n0 + 5), 1, rows(1), i * 2 + 2)

            ffn1_step(0, lambda s: None if s == 0 else NT)
            with pe.Fori(1, FF1_GROUPS // 2 - 1) as i:
                ffn1_step(i, lambda s: i * (2 * NT) + NT * s)
            i = FF1_GROUPS // 2 - 1
            up1(i, 2, 1, 1)
            down(n0 + 2, 4 * i + n0 + 3, 0, 2 * NT * i, 2 * i + 1)
            down(n0 + 3, 4 * i + n0 + 4, 1, 2 * NT * i + NT, 2 * i + 2)

            transposes(2)
            pe.wait_ge(ht_lo, 3 * KT)
            for u in range(2):
                unit_cm("pool", 0, 0, u)
            for u in range(2):
                unit_cm("q2", 0, 0, u)
            n, d = UNIT0["kv2"], USE0["kv2"]
            pe.wait_ge(lo_ready, n + 1)
            wait_pair("kv2", 0, 0, 0, d)
            for k in range(KT):
                wh, wl = rows_of(n % 2, KT, k, 0, P)
                mm3(bank(2 * (d % 2)), wh, wl, HTh[:, k, :], HTl[:, k, :], k == 0, k == KT - 1)
            for tt in range(NT):
                tok = slice(tt * P, (tt + 1) * P)
                for k in range(KT):
                    wh, wl = rows_of(n % 2, KT, k, P, P)
                    last = mm3(ps[:, 2 * (d % 2) + 1, tok], HTh[:, k, tok], HTl[:, k, tok], wh, wl,
                               k == 0, k == KT - 1)
            last.then_inc(pair_full, 1)
            pe.wait_ge(pd_ready, 4)
            n, d = UNIT0["group"], USE0["group"]
            pe.wait_ge(lo_ready, n + 1)
            for use in range(2):
                wait_pair("group", 0, 0, 0, d + use)
                for c in range(2):
                    g = 2 * use + c
                    wh, wl = Wh[:, n % 2, g * P:(g + 1) * P], Wl[:, n % 2, g * P:(g + 1) * P]
                    last = mm3(bank(2 * ((d + use) % 2) + c), wh, wl, PDh[:, g, :], PDl[:, g, :], True, True)
                last.then_inc(pair_full, 1)
            for par in range(2):
                pe.wait_ge(pair_taken[par], (USE0["gatep"] + 1 - par) // 2)
            pe.wait_ge(kd_in, 32)
            attention(att[1])
            pe.wait_ge(o_taken, len(items1) + len(items2))
            for name in ("gatep", "gatea"):
                for i in range(2):
                    unit_cm(name, i, 2, 0)
                    unit_cm(name, i, 2, 1)
            for u in range(2):
                unit_cm("poolb", 0, 0, u, act=(YPh, YPl), kts=4, dj=2 * u)
            pe.wait_ge(split_lo, 3)
            for u in range(2):
                unit_cm("attnb", 0, 0, u, act=(O2h, O2l), kts=4, dj=2 * u)
            pe.wait_ge(merged_lo, 2)
            tok_major_out("wout2", 1)
            transposes(3)
            pe.wait_ge(ht_lo, 4 * KT)
            m0 = UNIT0["ffn2"]
            R0, H0 = NT * FF1_GROUPS, FF1_GROUPS

            def up2(i, j, k):
                for v in range(2):
                    n = m0 + k + v
                    pe.wait_ge(lo_ready, i * 6 + (n + 1))
                    d = USE0["ffn2"] + 2 * j + v
                    wait_pair("ffn2", i, 4, 0, d)
                    for c in range(2):
                        for kt in range(KT):
                            wh, wl = rows_of(n % 2, KT, kt, c * P, P)
                            last = mm3(bank(2 * (d % 2) + c), wh, wl, HTh[:, kt, :], HTl[:, kt, :],
                                       kt == 0, kt == KT - 1)
                    last.then_inc(pair_full, 1)

            up2(0, 0, 0)
            with pe.Fori(0, FF2_GROUPS // 2) as i:
                up2(i, 1, 2)
                down(m0 + 4, i * 6 + (m0 + 5), 0, i * (2 * NT) + R0, i * 2 + (H0 + 1))
                up2(i, 2, 5)
                down(m0 + 7, i * 6 + (m0 + 8), 1, i * (2 * NT) + (R0 + NT), i * 2 + (H0 + 2))
            i = FF2_GROUPS // 2
            down(m0 + 2 + 6 * i, m0 + 6 * i + 3, 0, R0 + 2 * NT * i, H0 + 2 * i + 1)

        @block.scalar
        def _(act):
            order = Order(act, act_order)
            actf = nc.scalar.activation

            def square_sums(src, k, ready, count):
                for tt in range(NT):
                    order(actf(JUNK[:], src[:, tt, :], ACT.Square, accum_out=stat[:, tt:tt + 1]))
                actf(stat[:, 4:8], stat[:, 0:4], ACT.Sqrt, scale=1.0 / D,
                     bias=C[:, CC["eps"]:CC["eps"] + 1]).then_inc(ready, 1)

            def split_transposed(k, gain):
                for kt in range(KT):
                    act.wait_ge(ht_full, KT * k + kt + 1)
                    actf(HTh[:, kt, :], bank(4 + kt % 4), ACT.Copy, scale=pcol(gain, kt)).then_inc(ht_hi, 1)

            def evac_cols(name, i, per, j, dst, func=ACT.Copy, bias=None, scale=1.0, dst_per=2):
                d = USE0[name] + j
                act.wait_ge(pair_full, i * per + (d + 1))
                b = 2 * (d % 2)
                if bias is None:
                    last = actf(dst, ps[:, b:b + 2, :], func, scale=scale)
                else:
                    for c in range(2):
                        last = actf(dst[:, c, :], bank(b + c), func, bias=bias(c))
                last.then_inc(pair_taken[d % 2], 1)

            def attention(a):
                items, first, LG, PT = a["items"], a["first"], a["LG"], a["PT"]
                for i, it in enumerate(items):
                    act.wait_ge(nmx_ready, first + i + 1)
                    st = 16 + 8 * (i % 2)
                    if "sink" in it:
                        order(actf(stat[:, st + 3:st + 4], SNK[:, it["sink"]:it["sink"] + 1], ACT.Exp,
                                   bias=stat[:, st + 1:st + 2]))
                    actf(LG[:, i % 2, 0:it["n"]], LG[:, i % 2, 0:it["n"]], ACT.Exp, bias=stat[:, st + 1:st + 2],
                         accum_out=stat[:, st + 2:st + 3]).then_inc(exp_ready, 1)
                    for c, (v0, nv) in enumerate(it["chunks"]):
                        g = it["chunk0"] + c
                        act.wait_ge(pt_full, g + 1)
                        if c == 0 and first + i:
                            act.wait_ge(pv_full, first + i)
                        actf(PT[:, v0:v0 + nv, :].rearrange("p a b -> p (a b)"), bank(7 - 4 * (g % 2), nv * P),
                             ACT.Copy).then_inc(pt_taken, 1)
                    act.wait_ge(pv_full, first + i + 1)
                    actf(it["out"], ps[it["rows"], 2, 0:P], ACT.Copy).then_inc(o_taken, 1)

            act.wait_ge(rows_full, 1)
            order(actf(RROW[:, :, 0:T], ps[0:4, 4:7, :], ACT.Copy))
            actf(RROW[:, :, T:TOE_LEN], ps[0:4, 7, 0:3 * P].rearrange("h (g c) -> h g c", g=3),
                 ACT.Copy).then_inc(rows_ready, 1)
            act.wait_ge(rows_ready, 1)
            act.dma_start(toe_dram, RROW[:]).then_inc(toe_stored, 16)
            act.wait_ge(toe_stored, 16)
            act.dma_start(bass.AP(toe_skew.tensor, 0, [[TOE_LEN + 1, P], [SKEW, 12], [1, TOE_LEN]]),
                          bass.AP(toe_dram.tensor, 0, [[0, P], [TOE_LEN, 12], [1, TOE_LEN]])).then_inc(toe_skewed, 16)
            act.wait_ge(toe_skewed, 16)
            act.dma_start(TOE[:], bass.AP(toe_skew.tensor, P - 1, [[TOE_LEN, P], [SKEW, 12], [1, T]])
                          ).then_inc(toe_in, 16)

            act.wait_ge(x_in, 16)
            act.wait_ge(consts_in, 16)
            act.wait_ge(params_in, 16)
            square_sums(Xr, 0, rms_ready, 1)
            split_transposed(0, "mix_pre")
            evac_cols("qk", 0, 2, 0, QK[:, 0:2, :])
            evac_cols("qk", 0, 2, 1, QK[:, 2:4, :])
            with act.Fori(1, 3) as i:
                evac_cols("qk", i, 2, 0, QK[:, bass.ds(i * 4, 2), :])
                evac_cols("qk", i, 2, 1, QK[:, bass.ds(i * 4 + 2, 2), :])
            for u in range(3):
                d = USE0["v"] + u
                act.wait_ge(pair_full, d + 1)
                actf(V1[:, :, 256 * u:256 * u + 256],
                     ps[:, 2 * (d % 2):2 * (d % 2) + 2, :].rearrange("p a (b c) -> p (a b) c", b=2),
                     ACT.Copy).then_inc(pair_taken[d % 2], 1)
            d = USE0["lora"]
            act.wait_ge(pair_full, d + 1)
            actf(LRAW[:, :, 1:T + 1], ps[:, 2 * (d % 2):2 * (d % 2) + 2, :], ACT.Copy
                 ).then_inc(pair_taken[d % 2], 1)
            act.wait_ge(lora_shifted, 1)
            actf(FWA[0:HD, 0, :], LTMP[0:HD, 0, :], ACT.Tanh).then_inc(lora_act, 1)
            actf(FWA[HD:P, 0, :], LTMP[HD:P, 0, :], ACT.Copy).then_inc(lora_act, 1)
            actf(FWA[:, 1, :], LTMP[:, 1, :], ACT.Sigmoid).then_inc(lora_act, 1)
            attention(att[0])

            with act.Fori(0, 4) as q:
                act.wait_ge(pair_open, q * 2 + 1)
                act.dma_start(LWA[:], lora_wa[:, bass.ds(q * 256, 256)]).then_inc(lora_w_in, 16)
                act.dma_start(LGW[:], lora_g[:, bass.ds(q * 256, 256)]).then_inc(lora_w_in, 16)
                for j in range(3):
                    d = USE0["rwkv"] + j
                    act.wait_ge(pair_full, q * 4 + (d + 1))
                    actf(RAW[:, j, :, 1:T + 1], ps[:, 2 * (d % 2):2 * (d % 2) + 2, :], ACT.Copy
                         ).then_inc(pair_taken[d % 2], 1)
                d = USE0["rwkv"]
                act.wait_ge(pair_full, q * 4 + (d + 4))
                b = 2 * ((d + 3) % 2)
                for c in range(2):
                    last = actf(G1[:, bass.ds(q * 2 + c, 1), :].rearrange("p a t -> p (a t)"), bank(b + c),
                                ACT.Sigmoid, bias=pcol_dyn("b_gate", q * 2 + (KT + c)))
                last.then_inc(pair_taken[(d + 3) % 2], 1)
                for pp in range(2):
                    def w(name, m, k, pp=pp):
                        act.wait_ge(rs[name], q * (2 * m) + (m * pp + k))

                    def inc(ins, name):
                        ins.then_inc(rs[name], 1)

                    w("z_full", 1, 1)
                    actf(SZ[:], bank(4), ACT.Sigmoid, bias=pcol_dyn("w0", q * 2 + pp))
                    actf(Ab[:], bank(5), ACT.Sigmoid, bias=pcol_dyn("a0", q * 2 + pp))
                    inc(actf(Gb[:], bank(6), ACT.Copy), "z_read")
                    w("nrm_ready", 1, 1)
                    inc(actf(E[:], E[:], ACT.Sqrt), "sqrt_ready")
                    w("csm_ready", 1, 1)
                    actf(LM[:, 0, :], CS[:].rearrange("p (t c) -> p t c", c=P)[:, :, HD - 1], ACT.Exp, scale=-KAPPA)
                    actf(X2[:], E[:], ACT.Exp, scale=KAPPA)
                    actf(E[:], E[:], ACT.Exp, scale=-KAPPA)
                    inc(actf(T1[:], T1[:], ACT.Exp, scale=-KAPPA), "exps_ready")
                    for k, (b, dst) in enumerate(((5, TV), (6, TK), (7, TB))):
                        w("tok_full", 3, k + 1)
                        inc(actf(dst[:].rearrange("p a b -> p (a b)"), bank(b), ACT.Copy), "tok_ready")
                    nl = len(LEVELS)
                    for lv in range(1, nl):
                        for h in range(2):
                            w("tt_full", 2 * (nl - 1), 2 * (lv - 1) + h + 1)
                            last = actf(TT[h][:].rearrange("p a b -> p (a b)"), bank(6 + h), ACT.Copy)
                            if lv == nl - 1:
                                inc(last, "tt_last")
                            else:
                                inc(actf(Tb[h][:].rearrange("p a b -> p (a b)"), bank(4 + h), ACT.Copy), "t_ready")
                    for t in range(NT):
                        w("rhs_full", NT, t + 1)
                        inc(actf(RH[:].rearrange("p (h c) -> p h c", h=2), ps[:, 4:6, 0:HD], ACT.Copy), "rhs_ready")
                    w("y_full", 1, 1)
                    inc(actf(E[:], bank(6), ACT.Copy), "yraw_ready")
                    w("var_full", 1, 1)
                    inc(actf(X2[:], bank(5), ACT.Sqrt, scale=1.0 / HD, bias=C[:, CC["ln_eps"]:CC["ln_eps"] + 1]),
                        "std_ready")

            act.wait_ge(pair_open, PAIRS + 1)
            actf(OAh[:], OAT[:], ACT.Copy).then_inc(split_hi, 1)
            actf(ORh[:], ORW[:], ACT.Copy).then_inc(split_hi, 1)
            for u in range(4):
                evac_cols("gate0", 0, 0, u, MG[:, 2 * u:2 * u + 2, :], ACT.Sigmoid,
                          bias=lambda c, u=u: pcol("b_gate", 2 * u + c))
            act.dma_start(GN[:], post_gains[0]).then_inc(gain_in, 16)
            act.wait_ge(split_lo, 2)
            act.dma_start(Xr[:], x.rearrange("(t p) d -> p t d", p=P)).then_inc(x_back, 16)

            def merged_and_out(k, name, M):
                act.wait_ge(merged_hi, 2 * k + 1)
                actf(HTh[:], M[:], ACT.Copy).then_inc(merged_hi, 1)
                for u in range(4):
                    d = USE0[name] + u
                    act.wait_ge(pair_full, d + 1)
                    tt = 2 * (u % 2)
                    actf(Y[:, tt:tt + 2, 512 * (u // 2):512 * (u // 2) + 512], ps[:, 2 * (d % 2):2 * (d % 2) + 2, :],
                         ACT.Copy).then_inc(pair_taken[d % 2], 1)

            merged_and_out(0, "wout", MG)
            for d in (USE0["wout"] + 2, USE0["wout"] + 3):
                act.wait_ge(pair_taken[d % 2], d // 2 + 1)
            square_sums(Y, 0, yrms_ready, 1)
            act.wait_ge(x_ready, 1)
            square_sums(Xr, 1, rms_ready, 2)
            act.dma_start(GN[:], post_gains[1]).then_inc(gain_in, 16)
            split_transposed(1, "ffn_pre")

            def hidden1(i, j):
                d = USE0["ffn"] + j
                act.wait_ge(pair_full, i * 2 + (d + 1))
                b = 2 * (d % 2)
                if not (isinstance(i, int) and i == 0 and j == 0):
                    act.wait_ge(hid_sq, i * 2 + j)
                actf(HR[:], ps[:, b:b + 2, :], ACT.Relu).then_inc(pair_taken[d % 2], 1)
                act.wait_ge(hid_sq, i * 2 + (j + 1))
                if not (isinstance(i, int) and i == 0):
                    act.wait_ge(row_full, i * (2 * NT) + (NT * (j - 1)))
                actf(HIh[:, j % 2, :, :], HR2[:], ACT.Copy).then_inc(hid_hi, 1)

            hidden1(0, 0)
            hidden1(0, 1)
            with act.Fori(1, FF1_GROUPS // 2) as i:
                hidden1(i, 0)
                hidden1(i, 1)
            act.wait_ge(row_taken, NT * FF1_GROUPS)
            square_sums(Y, 0, yrms_ready, 2)
            act.wait_ge(x_ready, 2)
            square_sums(Xr, 2, rms_ready, 3)
            split_transposed(2, "mix2")

            act.dma_start(SNK[:], sink).then_inc(sink_in, 16)
            act.dma_start(IC[:].rearrange("p w t -> p (w t)"), icount).then_inc(ic_in, 16)
            act.wait_ge(kraw_ready, 1)
            for u in range(2):
                evac_cols("pool", 0, 0, u, Zp[:, 2 * u:2 * u + 2, 16:16 + T])
            for u in range(2):
                evac_cols("q2", 0, 0, u, Q2[:, 2 * u:2 * u + 2, :], scale=HD ** -0.5)
            d = USE0["kv2"]
            act.wait_ge(pair_full, d + 1)
            b = 2 * (d % 2)
            order(actf(KD[0:HD, 0, :], ps[0:HD, b, :], ACT.Copy))
            order(actf(KD[HD:P, 1, :], ps[HD:P, b, :], ACT.Copy))
            act.dma_start(KD[HD:P, 0, :], KD[0:HD, 0, :]).then_inc(kd_in, 16)
            act.dma_start(KD[0:HD, 1, :], KD[HD:P, 1, :]).then_inc(kd_in, 16)
            actf(V2[:].rearrange("p a b -> p (a b)"), bank(b + 1), ACT.Copy).then_inc(pair_taken[d % 2], 1)
            for u in range(2):
                d = USE0["group"] + u
                act.wait_ge(pair_full, d + 1)
                for c in range(2):
                    g = 2 * u + c
                    last = actf(YPh[:, g, :], bank(2 * (d % 2) + c), ACT.Copy, scale=pcol("pool_scale", g))
                last.then_inc(split_hi, 1)
            act.wait_ge(sink_in, 16)
            attention(att[1])
            for u in range(4):
                evac_cols("gatep", 0, 0, u, MG2[:, 2 * u:2 * u + 2, :], ACT.Sigmoid)
            for u in range(4):
                evac_cols("gatea", 0, 0, u, G2[:, 2 * u:2 * u + 2, :], ACT.Sigmoid)
            actf(O2h[:], O2[:], ACT.Copy).then_inc(split_hi, 1)
            merged_and_out(1, "wout2", MG2)
            act.wait_ge(x_ready, 3)
            square_sums(Xr, 3, rms_ready, 4)
            act.dma_start(GN[:], post_gains[2]).then_inc(gain_in, 16)
            split_transposed(3, "ffn2")

            def hidden2(i, j):
                d = USE0["ffn2"] + 2 * j
                act.wait_ge(pair_full, i * 4 + (d + 1))
                b = 2 * (d % 2)
                act.wait_ge(hid_sq, i * 2 + (FF1_GROUPS + j))
                actf(HR[:], ps[:, b:b + 2, :], ACT.Sigmoid).then_inc(hid_raw, 1)
                act.wait_ge(hid_sq, i * 2 + (FF1_GROUPS + j + 1))
                act.wait_ge(row_full, i * (2 * NT) + (NT * (FF1_GROUPS + j - 2) + NT))
                actf(HIh[:, j % 2, :, :], HR2[:], ACT.Copy).then_inc(hid_hi, 1)

            with act.Fori(0, FF2_GROUPS // 2) as i:
                hidden2(i, 0)
                hidden2(i, 1)
            hidden2(FF2_GROUPS // 2, 0)
            act.wait_ge(x_ready, 4)
            square_sums(Xr, 4, rms_ready, 5)
            act.wait_ge(y_ready, 1)
            act.dma_start(out.rearrange("(t p) d -> p t d", p=P), Y[:]).then_inc(out_done, 16)
            act.wait_ge(out_done, 16)

        @block.vector
        def _(dve):
            order = Order(dve, dve_order)
            v = nc.vector

            def used(d):
                dve.wait_ge(pair_taken[d % 2], d // 2 + 1)

            def normalise(k):
                dve.wait_ge(rms_ready, k + 1)
                order(v.reciprocal(stat[:, 8:12], stat[:, 4:8]))
                for tt in range(NT):
                    v.tensor_scalar(Y[:, tt, :], Xr[:, tt, :], stat[:, 8 + tt:9 + tt], None,
                                    ALU.mult).then_inc(xn_ready, 1)

            def split_transposed(k, gain):
                for kt in range(KT):
                    dve.wait_ge(ht_hi, KT * k + kt + 1)
                    v.scalar_tensor_tensor(HTl[:, kt, :], bank(4 + kt % 4), pcol(gain, kt), f32(HTh[:, kt, :]),
                                           ALU.mult, ALU.subtract).then_inc(ht_lo, 1)

            def add_normed(k):
                dve.wait_ge(yrms_ready, k + 1)
                dve.wait_ge(gain_in, 16 * (k + 1))
                order(v.reciprocal(stat[:, 8:12], stat[:, 4:8]))
                for tt in range(NT):
                    order(v.scalar_tensor_tensor(Y[:, tt, :], Y[:, tt, :], stat[:, 8 + tt:9 + tt], GN[:],
                                                 ALU.mult, ALU.mult))
                v.tensor_tensor(Xr[:], Xr[:], Y[:], ALU.add).then_inc(x_ready, 1)
                dve.wait_ge(x_ready, [1, 2][k])

            def attention(a):
                items, first, LG = a["items"], a["first"], a["LG"]
                for i, it in enumerate(items):
                    st = 16 + 8 * (i % 2)
                    mx, nmx, total, es, rec = (stat[:, st + c:st + c + 1] for c in range(5))
                    dve.wait_ge(lg_full, first + i + 1)
                    if i >= 2:
                        dve.wait_ge(pt_full, items[i - 2]["chunk1"])
                    for s in it["segs"]:
                        dst = LG[:, i % 2, s["off"]:s["off"] + s["n"]]
                        if "slope" in s:
                            ins = v.scalar_tensor_tensor(dst, s["bias"], s["slope"], bank(s["bank"], s["n"]),
                                                         ALU.mult, ALU.add)
                        else:
                            ins = v.scalar_tensor_tensor(dst, bank(s["bank"], s["n"]), HD ** -0.5, s["bias"],
                                                         ALU.mult, ALU.add)
                    ins.then_inc(lg_read, 1)
                    dve.wait_ge(lg_read, first + i + 1)
                    order(v.reduce_max(mx, LG[:, i % 2, 0:it["n"]], AX.X))
                    if "sink" in it:
                        order(v.tensor_tensor(mx, mx, SNK[:, it["sink"]:it["sink"] + 1], ALU.max))
                    v.tensor_scalar(nmx, mx, -1.0, None, ALU.mult).then_inc(nmx_ready, 1)
                    dve.wait_ge(exp_ready, first + i + 1)
                    if "sink" in it:
                        order(v.tensor_tensor(total, total, es, ALU.add))
                    order(v.reciprocal(rec, total))
                    v.tensor_scalar(LG[:, i % 2, 0:it["n"]], LG[:, i % 2, 0:it["n"]], rec, None,
                                    ALU.mult).then_inc(prob_ready, 1)

            v.memset(RB[N_BUCKETS:N_BUCKETS + 1, :], NEG).then_inc(rb_ready, 1)
            dve.wait_ge(params_in, 16)
            dve.wait_ge(x_in, 16)
            normalise(0)
            split_transposed(0, "mix_pre")
            dve.wait_ge(toe_stored, 16)
            order(v.memset(LRAW[:, :, 0:1], 0.0))
            used(USE0["lora"])
            order(v.tensor_tensor(LTMP[:], LRAW[:, :, 0:T], LRAW[:, :, 1:T + 1], ALU.subtract))
            for c in range(2):
                last = v.scalar_tensor_tensor(LTMP[:, c, :], LTMP[:, c, :], pcol("mu", 24 + c), LRAW[:, c, 1:T + 1],
                                              ALU.mult, ALU.add)
            last.then_inc(lora_shifted, 1)
            dve.wait_ge(lora_act, 3)
            attention(att[0])
            dve.wait_ge(o_taken, len(items1))
            for h in range(2):
                order(v.memset(GM[h][:], 0.0))
            order(v.memset(RAW[:, :, :, 0:1], 0.0))
            dve.sem_inc(pair_open, 1)

            mask = C[:, CC["strict_incl"]:CC["strict_incl"] + 2 * P].bitcast(I32)

            def cast4(ap):
                return ap.unsqueeze(1).to_broadcast([P, NT, P])

            with dve.Fori(0, 4) as q:
                o = Order(dve, dve_rwkv, q * DVE_STEPS)
                for j in (1, 2):
                    d = USE0["rwkv"] + j
                    dve.wait_ge(pair_taken[d % 2], q * 2 + (d // 2 + 1))
                for pp in range(2):
                    def w(name, m, k, pp=pp):
                        dve.wait_ge(rs[name], q * (2 * m) + (m * pp + k))

                    def inc(ins, name):
                        ins.then_inc(rs[name], 1)

                    rr, kk_, vv = (RAW[:, j, pp, 1:T + 1] for j in range(3))
                    pcol_p = lambda name, k=0, pp=pp: pcol_dyn(name, q * 2 + (pp + k))
                    dve.wait_ge(pair_open, q * 2 + (pp + 1))
                    for j, f in enumerate((rr, kk_, vv)):
                        o(v.tensor_tensor(T1[:], RAW[:, j, pp, 0:T], f, ALU.subtract))
                        o(v.scalar_tensor_tensor(f, T1[:], pcol_p("mu", 8 * j), f, ALU.mult, ALU.add))
                    o(v.tensor_scalar(KK[:], kk_, pcol_p("k_k"), None, ALU.mult))
                    inc(v.tensor_tensor(X2[:], KK[:], KK[:], ALU.mult), "sq_ready")
                    w("z_read", 1, 1)
                    o(v.tensor_scalar(T1[:], Ab[:], -1.0, pcol_p("k_a"), ALU.add, ALU.mult))
                    o(v.scalar_tensor_tensor(kk_, T1[:], 1.0, kk_, ALU.add, ALU.mult))
                    inc(v.scalar_tensor_tensor(T1[:], rr, pcol_p("r_k"), kk_, ALU.mult, ALU.mult), "rk_ready")
                    w("ss_full", 1, 1)
                    inc(v.tensor_scalar(E[:], bank(7), L2_EPS2, None, ALU.max), "nrm_ready")
                    for t in range(NT):
                        ins = v.tensor_tensor_scan(CS[:, t * P:(t + 1) * P], ones, SZ[:, t * P:(t + 1) * P], 0.0,
                                                   ALU.mult, ALU.add)
                    o(ins)
                    w("sqrt_ready", 1, 1)
                    o(v.reciprocal(E[:], E[:]))
                    o(v.tensor_tensor(KK[:], KK[:], E[:], ALU.mult))
                    o(v.tensor_tensor(Ab[:], Ab[:], KK[:], ALU.mult))
                    cs4 = CS[:].rearrange("p (t c) -> p t c", c=P)
                    o(v.tensor_tensor(E[:].rearrange("p (t c) -> p t c", c=P), cs4,
                                      cs4[:, :, HD - 1:HD].to_broadcast([P, NT, P]), ALU.subtract))
                    w("bonus_full", 1, 1)
                    inc(v.tensor_tensor(T1[:], E[:], SZ[:], ALU.subtract), "csm_ready")
                    dve.wait_ge(rs["csm_ready"], q * 2 + (pp + 1))
                    o(v.tensor_tensor(SZ[:], bank(4), vv, ALU.mult))
                    w("exps_ready", 1, 1)
                    as4 = lambda ap: ap.rearrange("p (t c) -> p t c", c=P)
                    v.tensor_tensor(RA[:, :, 0, :], as4(rr), as4(E[:]), ALU.mult)
                    v.scalar_tensor_tensor(RA[:, :, 1, :], as4(KK[:]), -1.0, as4(T1[:]), ALU.mult, ALU.mult)
                    v.tensor_tensor(KB[:, 0, :], kk_, X2[:], ALU.mult)
                    inc(v.tensor_tensor(KB[:, 1, :], Ab[:], X2[:], ALU.mult), "rakb_ready")
                    o(v.tensor_tensor(LM[:, 1, 0:NT - 1], as4(E[:])[:, 0:NT - 1, P - 1], LM[:, 0, 1:NT], ALU.mult))
                    inc(v.memset(S[:], 0.0), "s_ready")
                    for t in range(NT):
                        w("gram_full", NT, t + 1)
                        v.memset(stat[:, 40 + t:41 + t], 0.0)
                        for h in range(2):
                            ins = v.copy_predicated(GM[h][:, t, :, :].rearrange("p (a b) c -> p a (b c)", a=2),
                                                    mask.unsqueeze(1).to_broadcast([P, 2, 2 * P]),
                                                    ps[:, 4 + 2 * (t % 2) + h, :].rearrange("p (a b) -> p a b", a=2))
                        inc(ins, "gram_taken")
                    w("gram_taken", NT, NT)
                    nl = len(LEVELS)
                    lmask = lambda lv: cast4(C[:, CC["levels"] + lv * P:CC["levels"] + (lv + 1) * P])
                    b3 = lambda b: ps[:, b, :].rearrange("p (t c) -> p t c", c=P)
                    for h in range(2):
                        inc(v.tensor_tensor(Mb[h][:], GM[h][:, :, 3, :], lmask(0), ALU.mult), "m_ready")
                    for h in range(2):
                        w("m_ready", 2 * nl, h + 1)
                        o(v.tensor_tensor(TT[h][:], Mb[h][:], cast4(ident), ALU.add))
                        w("x_full", 2 * nl, h + 1)
                        inc(v.tensor_tensor(Tb[h][:], b3(4 + h), cast4(ident), ALU.add), "t2_ready")
                        inc(v.tensor_tensor(Mb[h][:], GM[h][:, :, 3, :], lmask(1), ALU.mult), "m_ready")
                    for lv in range(1, nl):
                        for h in range(2):
                            w("x_full", 2 * nl, 2 * lv + h + 1)
                            inc(v.tensor_tensor(Xb[h][:], b3(4 + h), cast4(ident), ALU.add), "x1_ready")
                            if lv + 1 < nl:
                                inc(v.tensor_tensor(Mb[h][:], GM[h][:, :, 3, :], lmask(lv + 1), ALU.mult), "m_ready")
                    for t in range(NT):
                        w("sa_full", NT, t + 1)
                        inc(v.tensor_copy(SA[:], ps[:, 4, P:2 * P]), "sa_ready")
                        if t < NT - 1:
                            w("s_full", NT - 1, t + 1)
                            o(v.tensor_tensor(S[:], ps[:, 5, P:P + HD], S[:], ALU.add))
                            inc(v.tensor_scalar(S[:], S[:], LM[:, 1, t:t + 1], None, ALU.mult), "s_ready")
                    w("mu_full", 1, 1)
                    o(v.scalar_tensor_tensor(T1[:], bank(4), -1.0 / HD, E[:], ALU.mult, ALU.add))
                    inc(v.tensor_tensor(X2[:], T1[:], T1[:], ALU.mult), "ysq_ready")
                    w("std_ready", 1, 1)
                    o(v.reciprocal(X2[:], X2[:]))
                    o(v.tensor_tensor(T1[:], T1[:], X2[:], ALU.mult))
                    o(v.tensor_scalar(T1[:], T1[:], pcol_p("ln_w"), pcol_p("ln_b"), ALU.mult, ALU.add))
                    o(v.tensor_tensor(T1[:], T1[:], SZ[:], ALU.add))
                    v.tensor_tensor(ORW[:, bass.ds(q * 2 + pp, 1), :].rearrange("p a t -> p (a t)"), T1[:], Gb[:],
                                    ALU.mult).then_inc(pair_open, 1)
                assert o.n == DVE_STEPS, o.n
            dve.wait_ge(pair_open, PAIRS + 1)

            dve.wait_ge(split_hi, 1)
            v.tensor_tensor(OAl[:], OAT[:], f32(OAh[:]), ALU.subtract).then_inc(split_lo, 1)
            dve.wait_ge(split_hi, 2)
            v.tensor_tensor(ORl[:], ORW[:], f32(ORh[:]), ALU.subtract).then_inc(split_lo, 1)

            def gate_times(name, uses, M, G=None, tmp=None):
                for u in range(uses):
                    d = USE0[name] + u
                    dve.wait_ge(pair_full, d + 1)
                    src = ps[:, 2 * (d % 2):2 * (d % 2) + 2, :]
                    m = M[:, 2 * u:2 * u + 2, :]
                    if G is None:
                        v.tensor_tensor(m, m, src, ALU.mult).then_inc(pair_taken[d % 2], 1)
                        dve.wait_ge(pair_taken[d % 2], d // 2 + 1)
                    else:
                        g = G[:, 2 * u:2 * u + 2, :]
                        v.tensor_tensor(g, g, src, ALU.mult).then_inc(pair_taken[d % 2], 1)
                        dve.wait_ge(pair_taken[d % 2], d // 2 + 1)
                        order(v.tensor_tensor(m, m, g, ALU.add))

            def merge_low(k, M):
                dve.sem_inc(merged_hi, 1)
                dve.wait_ge(merged_hi, 2 * k + 2)
                v.tensor_tensor(HTl[:], M[:], f32(HTh[:]), ALU.subtract).then_inc(merged_lo, 1)

            for d in (USE0["gate0"] + 2, USE0["gate0"] + 3):
                used(d)
            gate_times("attb", 4, MG)
            gate_times("rwkvb", 4, MG, G=G1)
            merge_low(0, MG)
            dve.wait_ge(x_back, 16)
            add_normed(0)
            normalise(1)
            split_transposed(1, "ffn_pre")
            order(v.memset(Y[:], 0.0))

            def add_rows(i, j, rows0):
                if rows0 or not (isinstance(i, int) and 2 * i + j == 0):
                    dve.wait_ge(row_taken, i * (2 * NT) + (rows0 + NT * j))
                for tt in range(NT):
                    dve.wait_ge(row_full, i * (2 * NT) + (rows0 + NT * j + tt + 1))
                    b = 4 + 2 * (tt % 2)
                    v.tensor_tensor(Y[:, tt, :].rearrange("p (a b) -> p a b", a=2), ps[:, b:b + 2, :],
                                    Y[:, tt, :].rearrange("p (a b) -> p a b", a=2), ALU.add).then_inc(row_taken, 1)

            def hidden1(i, j):
                d = USE0["ffn"] + j
                dve.wait_ge(pair_taken[d % 2], i + (d // 2 + 1))
                if not (isinstance(i, int) and 2 * i + j == 0):
                    dve.wait_ge(hid_lo, i * 2 + j)
                v.tensor_tensor(HR2[:], HR[:], HR[:], ALU.mult).then_inc(hid_sq, 1)
                dve.wait_ge(hid_hi, i * 2 + (j + 1))
                v.tensor_tensor(HIl[:, j % 2, :, :], HR2[:], f32(HIh[:, j % 2, :, :]), ALU.subtract).then_inc(hid_lo, 1)

            hidden1(0, 0)
            hidden1(0, 1)
            add_rows(0, 0, 0)
            with dve.Fori(1, FF1_GROUPS // 2) as i:
                hidden1(i, 0)
                add_rows(i, -1, 0)
                hidden1(i, 1)
                add_rows(i, 0, 0)
            add_rows(FF1_GROUPS // 2 - 1, 1, 0)
            add_normed(1)
            normalise(2)
            split_transposed(2, "mix2")

            v.memset(Zp[:], 0.0).then_inc(kraw_ready, 1)
            order(v.memset(PW[:], 0.0))
            used(USE0["pool"])
            used(USE0["pool"] + 1)
            dve.wait_ge(ic_in, 16)
            a0, b0 = 8, 8 + T + 16
            for g in range(4):
                cur = Zp[:, g, :]
                for lvl in range(g + 1):
                    left, right = (1, 0) if lvl == 0 else (2 ** (lvl - 1), 2 ** (lvl - 1))
                    dst = PW[:, lvl % 2, :]
                    order(v.tensor_tensor(dst[:, a0:b0], cur[:, a0 - left:b0 - left], cur[:, a0 + right:b0 + right],
                                          ALU.add))
                    cur = dst
                mean = PW[:, (g + 1) % 2, 16:16 + T]
                order(v.tensor_tensor(mean, cur[:, 16:16 + T], IC[:, g, :], ALU.mult))
                order(v.tensor_tensor(mean, mean, Zp[:, g, 16:16 + T], ALU.subtract))
                order(v.tensor_copy(PDh[:, g, :], mean))
                v.tensor_tensor(PDl[:, g, :], mean, f32(PDh[:, g, :]), ALU.subtract).then_inc(pd_ready, 1)
                dve.wait_ge(pd_ready, g + 1)
            for u in range(2):
                d = USE0["group"] + u
                dve.wait_ge(split_hi, 3 + u)
                for c in range(2):
                    g = 2 * u + c
                    last = v.scalar_tensor_tensor(YPl[:, g, :], bank(2 * (d % 2) + c), pcol("pool_scale", g),
                                                  f32(YPh[:, g, :]), ALU.mult, ALU.subtract)
                last.then_inc(pair_taken[d % 2], 1)
            dve.wait_ge(sink_in, 16)
            attention(att[1])
            for d in (USE0["gatea"] + 2, USE0["gatea"] + 3):
                used(d)
            dve.wait_ge(split_hi, 5)
            v.tensor_tensor(O2l[:], O2[:], f32(O2h[:]), ALU.subtract).then_inc(split_lo, 1)
            gate_times("poolb", 4, MG2)
            gate_times("attnb", 4, MG2, G=G2)
            merge_low(1, MG2)
            for d in (USE0["wout2"] + 2, USE0["wout2"] + 3):
                used(d)
            v.tensor_tensor(Xr[:], Xr[:], Y[:], ALU.add).then_inc(x_ready, 1)
            dve.wait_ge(x_ready, 3)
            normalise(3)
            split_transposed(3, "ffn2")
            order(v.memset(Y[:], 0.0))
            R0 = NT * FF1_GROUPS

            def hidden2(i, j):
                d = USE0["ffn2"] + 2 * j
                dve.wait_ge(hid_raw, i * 2 + (j + 1))
                dve.wait_ge(hid_lo, i * 2 + (FF1_GROUPS + j))
                b = 2 * (d % 2)
                v.tensor_tensor(HR2[:], ps[:, b:b + 2, :], HR[:], ALU.mult).then_inc(pair_taken[d % 2], 1)
                dve.wait_ge(pair_taken[d % 2], i * 2 + (d // 2 + 1))
                d += 1
                dve.wait_ge(pair_full, i * 4 + (d + 1))
                b = 2 * (d % 2)
                v.tensor_tensor(HR2[:], ps[:, b:b + 2, :], HR2[:], ALU.mult).then_inc(pair_taken[d % 2], 1)
                dve.wait_ge(pair_taken[d % 2], i * 2 + (d // 2 + 1))
                dve.sem_inc(hid_sq, 1)
                dve.wait_ge(hid_hi, i * 2 + (FF1_GROUPS + j + 1))
                v.tensor_tensor(HIl[:, j % 2, :, :], HR2[:], f32(HIh[:, j % 2, :, :]), ALU.subtract).then_inc(hid_lo, 1)

            hidden2(0, 0)
            hidden2(0, 1)
            add_rows(0, 0, R0)
            with dve.Fori(1, FF2_GROUPS // 2) as i:
                hidden2(i, 0)
                add_rows(i, -1, R0)
                hidden2(i, 1)
                add_rows(i, 0, R0)
            i = FF2_GROUPS // 2
            hidden2(i, 0)
            add_rows(i, -1, R0)
            add_rows(i, 0, R0)
            dve.wait_ge(row_taken, NT * (FF1_GROUPS + FF2_GROUPS))
            v.tensor_tensor(Xr[:], Xr[:], Y[:], ALU.add).then_inc(x_ready, 1)
            dve.wait_ge(rms_ready, 5)
            dve.wait_ge(gain_in, 48)
            order(v.reciprocal(stat[:, 8:12], stat[:, 4:8]))
            for tt in range(NT):
                last = v.scalar_tensor_tensor(Y[:, tt, :], Xr[:, tt, :], stat[:, 8 + tt:9 + tt], GN[:],
                                              ALU.mult, ALU.mult)
            last.then_inc(y_ready, 1)


def kernel(**inputs):
    import concourse.bacc as _bacc
    from concourse.bass_utils import run_bass_kernel_spmd as _run

    a = {k: np.asarray(v) for k, v in inputs.items()}
    w_in, w_in2 = a["w_in"][0], a["w_in_2"][0]

    def unit(w, kts):
        u = np.ascontiguousarray(w.reshape(kts, P, -1).transpose(1, 0, 2)).reshape(P, -1)
        return u if u.shape[1] == UNIT else np.concatenate([u, np.zeros((P, UNIT - u.shape[1]), u.dtype)], 1)

    def cols(w, c0, n, step=256, kts=KT):
        return [unit(w[:, c:c + step], kts) for c in range(c0, c0 + n, step)]

    def grid(w):
        return [unit(w[r:r + 512, c:c + 512], 4) for c in (0, 512) for r in (0, 512)]

    def ffn(ups, down, groups):
        out = []
        for g in range(groups + 1):
            if g < groups:
                out += [unit(u[:, 256 * g:256 * g + 256], KT) for u in ups]
            if g > 0:
                out.append(unit(down[256 * (g - 1):256 * g], 2))
        return out

    rk0 = 3 * ATT_W
    gate0 = rk0 + 3 * RW + 256
    units = cols(w_in, 0, 2 * ATT_W) + cols(w_in, 2 * ATT_W, ATT_W) + cols(w_in, rk0 + 3 * RW, 256)
    for q in range(4):
        units += [unit(w_in[:, c + 256 * q:c + 256 * q + 256], KT)
                  for c in (rk0, rk0 + RW, rk0 + 2 * RW, gate0 + D)]
    units += cols(w_in, gate0, D) + [unit(a["w_att_branch"][0], 2)] + cols(a["w_rwkv_branch"][0], 0, D)
    units += grid(a["w_out"][0]) + ffn([a["w_ffn1"][0]], a["w_ffn2"][0], FF1_GROUPS)
    units += cols(w_in2, 0, 512) + cols(w_in2, 512, 512) + cols(w_in2, 1024, 256)
    units += [unit(a["w_pool_group_2"][0].reshape(512, P), 4)]
    units += cols(w_in2, 1280, 2 * D)
    units += cols(a["w_pool_branch_2"][0], 0, D, 512, 4) + cols(a["w_attn_branch_2"][0], 0, D, 512, 4)
    units += grid(a["w_out_2"][0])
    units += ffn([a["w_ffn_gate_2"][0], a["w_ffn_up_2"][0]], a["w_ffn_down_2"][0], FF2_GROUPS)
    assert len(units) == N_UNITS, (len(units), N_UNITS)

    table = {"mu": "shift_mu", "w0": "w0", "a0": "a0", "k_k": "k_k", "k_a": "k_a", "r_k": "r_k", "ln_w": "ln_x_w",
             "ln_b": "ln_x_b", "b_gate": "b_gate", "mix_pre": "norm_mix_pre", "ffn_pre": "norm_ffn_pre",
             "mix2": "norm_mix_2", "ffn2": "norm_ffn_2", "pool_scale": "pool_scale_2"}
    params = np.concatenate([a[table[n]].reshape(-1, P) for n, _ in PCOLS]).T
    gains = np.stack([a["norm_mix_post"][0], a["norm_ffn_post"][0], a["norm_final_2"]])
    arrays = {
        "x": a["x"][0],
        "wpack": np.stack(units),
        "lora_wa": np.concatenate([a["w_w2"][0], a["w_a2"][0]]),
        "lora_g": a["w_g2"][0],
        "params": params,
        "rel_bias": a["rel_bias"],
        "post_gains": np.broadcast_to(gains[:, None, :], (3, P, D)),
        "sink": np.broadcast_to(a["sink_2"][0][None, :], (P, Q_HEADS2)),
        "ctab": constants(),
        "btab": bucket_table(),
        "icount": np.broadcast_to(inv_counts().reshape(1, -1), (P, 4 * T)),
    }
    nc = _bacc.Bacc("TRN2", target_bir_lowering=False, num_devices=1)
    feeds, args = {}, []
    for name, arr in arrays.items():
        arr = np.ascontiguousarray(arr)
        feeds[f"in_{name}"] = arr
        args.append(nc.dram_tensor(f"in_{name}", arr.shape, mybir.dt.from_np(arr.dtype), kind="ExternalInput").ap())
    args.append(nc.dram_tensor("out_x", (T, D), F32, kind="ExternalOutput").ap())
    build(nc, *args)
    r = _run(nc, [feeds], core_ids=[0])
    return r.results[0]["out_x"].reshape(1, T, D)
```

```python
import math
from contextlib import ExitStack

import numpy as np

import concourse.bass as bass
from concourse import mybir

F32 = mybir.dt.float32
F32R = mybir.dt.float32r
I32 = mybir.dt.int32
ACT = mybir.ActivationFunctionType
ALU = mybir.AluOpType
AX = mybir.AxisListType

P = 128
T = 512
NT = T // P
D = 1024
KT = D // P
HD = 64
UNIT = 2048
NEG = -1e30
KAPPA = math.exp(-0.5)
EPS = 1e-6
LN_EPS = 64e-5
L2_EPS2 = 1e-24

ATT_W = 768
N_GROUPS = 3
DILATIONS = (1, 4, 16)
KEYS = 128
N_BUCKETS = 32
MAX_DIST = KEYS * DILATIONS[-1]
RW = 1024
PAIRS = 8
FF1_GROUPS = 16
D_FF2 = 2816
FF2_GROUPS = D_FF2 // 256
POOL_W = 512
Q_HEADS2 = 8
LEVELS = (2, 4, 8, 16, 32, 64, 128)
DVE_STEPS = 48

STAGES = [("qk", 6), ("v", 3), ("lora", 1), ("rwkv", 16), ("gate0", 4), ("attb", 1), ("rwkvb", 4),
          ("wout", 4), ("ffn", 2 * FF1_GROUPS), ("pool", 2), ("q2", 2), ("kv2", 1), ("group", 1),
          ("gatep", 4), ("gatea", 4), ("poolb", 2), ("attnb", 2), ("wout2", 4), ("ffn2", 3 * FF2_GROUPS)]
USES = dict(qk=6, v=3, lora=1, gate0=4, attb=4, rwkv=0, rwkvb=4, wout=4, ffn=FF1_GROUPS, pool=2, q2=2,
            kv2=1, gatep=4, gatea=4, group=2, poolb=4, attnb=4, wout2=4, ffn2=2 * FF2_GROUPS)
UNIT0, USE0 = {}, {}
_n = _d = 0
for _name, _count in STAGES:
    UNIT0[_name], USE0[_name] = _n, _d
    _n += _count
    _d += USES[_name]
N_UNITS = _n

PCOLS = [("mu", 26), ("w0", 8), ("a0", 8), ("k_k", 8), ("k_a", 8), ("r_k", 8), ("ln_w", 8), ("ln_b", 8),
         ("b_gate", 16), ("mix_pre", 8), ("ffn_pre", 8), ("mix2", 8), ("ffn2", 8), ("pool_scale", 4)]
PC = {}
_c = 0
for _name, _count in PCOLS:
    PC[_name] = _c
    _c += _count
N_PCOLS = _c

CCOLS = [("ident", P), ("ones_head", P), ("ones", P), ("strict_incl", 2 * P), ("levels", len(LEVELS) * P),
         ("absdist", 3 * P), ("eps", 1), ("ln_eps", 1)]
CC = {}
_c = 0
for _name, _count in CCOLS:
    CC[_name] = _c
    _c += _count
N_CCOLS = _c
TOE_LEN = 640


def constants():
    p = np.arange(P)[:, None]
    c = np.arange(P)[None, :]
    tab = np.zeros((P, N_CCOLS), np.float32)

    def put(name, a):
        tab[:, CC[name]:CC[name] + a.shape[1]] = a

    put("ident", (p == c).astype(np.float32))
    put("ones_head", (p // HD == c // HD).astype(np.float32))
    put("ones", np.ones((P, P), np.float32))
    put("strict_incl", np.concatenate([(p <= c), (p < c)], 1).astype(np.float32))
    put("levels", np.concatenate([((p // b == c // b) & (p % b < b // 2) & (c % b >= b // 2))
                                  for b in LEVELS], 1).astype(np.float32))
    x = np.arange(3 * P)[None, :]
    dist = np.abs(p - (x - P))
    put("absdist", np.where(dist <= P, dist, 1e30).astype(np.float32))
    put("eps", np.full((P, 1), EPS, np.float32))
    put("ln_eps", np.full((P, 1), LN_EPS, np.float32))
    return tab


def bucket_table():
    out = np.zeros((N_BUCKETS + 1, N_GROUPS * TOE_LEN), np.float32)
    exact = N_BUCKETS // 2
    for g, d in enumerate(DILATIONS):
        for v in range(TOE_LEN):
            dist = T - 1 - v
            row = N_BUCKETS
            if dist >= 0 and dist % d == 0 and dist // d <= KEYS:
                if dist < exact:
                    row = dist
                else:
                    big = exact + int(np.float32(np.log(np.float32(dist) / np.float32(exact)))
                                      / np.float32(math.log(MAX_DIST / exact)) * np.float32(N_BUCKETS - exact))
                    row = min(big, N_BUCKETS - 1)
            out[row, g * TOE_LEN + v] = 1.0
    return out


def inv_counts():
    t = np.arange(T)
    rows = []
    for w in (2, 4, 8, 16):
        n = np.clip(t + w // 2, 0, T) - np.clip(t - w // 2, 0, T)
        rows.append(1.0 / n.astype(np.float32))
    return np.stack(rows).astype(np.float32)



def build(nc, x, wpack, lora_wa, lora_g, params, rel_bias, post_gains, sink, ctab, btab, icount, out):
    toe_dram = nc.dram_tensor("bias_rows_dram", (4, N_GROUPS, TOE_LEN), F32, kind="Internal").ap()
    SKEW = P * (TOE_LEN + 1)
    gate1_dram = nc.dram_tensor("gate1_dram", (PAIRS, P, T), F32, kind="Internal").ap()
    toe_skew = nc.dram_tensor("bias_skewed_dram", (12, SKEW), F32, kind="Internal").ap()

    with ExitStack() as ctx:
        top = [nc.sbuf_base + (-nc.sbuf_base) % 64]

        def place(name, shape, dt=F32, at=None):
            size = 4 * int(np.prod(shape[1:]))
            if at is None:
                at = top[0]
                top[0] += size + (-size) % 64
            return nc.alloc_sbuf_tensor_at(name, shape, dt, offset=at), at + size + (-size) % 64

        def fixed(name, shape, dt=F32):
            return place(name, shape, dt)[0]

        class Region:

            def __init__(self, at):
                self.at = at

            def __call__(self, name, shape, dt=F32):
                t, self.at = place(name, shape, dt, self.at)
                assert self.at <= nc.sbuf_usable_end, (name, self.at - nc.sbuf_usable_end)
                return t

        def sem(name):
            return ctx.enter_context(nc.semaphore(name))

        Xr = fixed("x_res", [P, NT, D])
        x_at = top[0] - 4 * NT * D
        Y = fixed("y_tok", [P, NT, D])
        y_at = top[0] - 4 * NT * D
        HTh = fixed("ht_hi", [P, KT, T], F32R)
        HTl = fixed("ht_lo", [P, KT, T], F32R)
        raw = fixed("w_raw", [P, 2, UNIT])
        Wh = fixed("w_hi", [P, 2, UNIT], F32R)
        Wl = fixed("w_lo", [P, 2, UNIT], F32R)
        C = fixed("consts", [P, N_CCOLS])
        PR = fixed("params_sb", [P, N_PCOLS])
        stat = fixed("stat", [P, 64])
        OAT = fixed("att_out", [P, 2, T])
        FWA = fixed("lora_in", [P, 2, T])
        base = top[0]

        r = Region(base)
        QK = r("qk_t", [P, 12, T])
        V1 = r("v_tok", [P, NT, ATT_W])
        TOE = r("toe", [P, 12, T])
        LG1 = r("logits1", [P, 2, 1280])
        PT1 = r("probs_t1", [P, 10, P])
        r = Region(base)
        RB = r("rel_bias_sb", [N_BUCKETS + 1, 12])
        BT = r("buckets_sb", [N_BUCKETS + 1, N_GROUPS * TOE_LEN])
        RROW = r("bias_rows", [4, N_GROUPS, TOE_LEN])
        r = Region(base + 4 * (12 * T + NT * ATT_W + 12 * T))
        LRAW = r("lora_raw", [P, 2, T + 1])
        LTMP = r("lora_tmp", [P, 2, T])
        ORW = place("rwkv_out", [P, PAIRS, T], at=x_at)[0]
        G1 = place("gate1", [P, KT, T], at=y_at)[0]
        r = Region(y_at)
        RA = [r(f"ra{i}", [P, NT, 2, P]) for i in range(2)]
        BON = [r(f"bonus{i}", [P, T]) for i in range(2)]
        GT = r("gate1_tile", [P, T])
        identR = r("ident_r", [P, P], F32R)
        S = r("state", [P, HD])
        RH = r("rhs_sb", [P, P])
        SA = r("sa_sb", [P, P])
        LM = r("mid_decay", [P, 2, 2, NT])
        assert r.at <= y_at + 4 * NT * D
        r = Region(base)
        TF = [r(f"tinv_full{h}", [P, NT, P]) for h in range(2)]
        LW = [r(f"lora_w{i}", [P, 2, P]) for i in range(2)]
        RAW = r("rkv", [P, 2, 3, T + 1])
        Gb = [r(f"rwkv_gate{i}", [P, T]) for i in range(2)]
        SZ = r("sig_w", [P, T])
        Ab = r("iclr", [P, T])
        CS = r("cum_decay", [P, T])
        KK = r("kk", [P, T])
        E = r("work_e", [P, T])
        T1 = r("work_t", [P, T])
        X2 = r("work_x", [P, T])
        KB = r("kb", [P, 2, T])
        TV = r("v_chunk", [P, NT, P])
        TK = r("k_chunk", [P, NT, P])
        TB = r("b_chunk", [P, NT, P])
        GM = [r(f"gram{h}", [P, NT, 4, P]) for h in range(2)]
        Mb = [r(f"level{h}", [P, NT, P], F32R) for h in range(2)]
        Xb = [r(f"xinv{h}", [P, NT, P], F32R) for h in range(2)]
        Tb = [r(f"tinv{h}", [P, NT, P], F32R) for h in range(2)]
        TT = [r(f"tinv_t{h}", [P, NT, P], F32R) for h in range(2)]
        K16 = 4 * KT * T
        MG = place("merged", [P, KT, T], at=base)[0]
        ORh = place("rwkv_hi", [P, KT, T], F32R, at=base + K16)[0]
        ORl = place("rwkv_lo", [P, KT, T], F32R, at=base + 2 * K16)[0]
        OAh = place("att_hi", [P, 2, T], F32R, at=base + 3 * K16)[0]
        OAl = place("att_lo", [P, 2, T], F32R, at=base + 3 * K16 + K16 // 4)[0]
        GN = place("gains", [P, D], at=base + 4 * K16)[0]
        JUNK = place("squares", [P, D], at=base + 4 * K16 + K16 // 4)[0]
        r = Region(base)
        HIh = r("hid_hi", [P, 2, 2, T], F32R)
        HIl = r("hid_lo", [P, 2, 2, T], F32R)
        HR = r("hid_raw", [P, 2, T])
        HR2 = r("hid_sq", [P, 2, T])
        r = Region(base)
        Zp = r("pool_z", [P, 4, T + 32])
        Q2 = r("q2_t", [P, 4, T])
        KD = r("k2_t", [P, 2, T])
        V2 = r("v2_tok", [P, NT, P])
        pd_at = r.at
        PDh = r("pool_hi", [P, 4, T], F32R)
        PDl = r("pool_lo", [P, 4, T], F32R)
        YPh = r("yp_hi", [P, 4, T], F32R)
        YPl = r("yp_lo", [P, 4, T], F32R)
        O2 = r("att2_out", [P, 4, T])
        LG2 = r("logits2", [P, 2, 3 * P])
        PT2 = r("probs_t2", [P, 3, P])
        SNK = r("sink_sb", [P, Q_HEADS2])
        PW = r("pool_tmp", [P, 2, T + 32])
        IC = place("icount_sb", [P, 4, T], at=y_at)[0]
        MG2 = place("merged2", [P, KT, T], at=base)[0]
        G2 = place("gate_att2", [P, KT, T], at=pd_at)[0]
        O2h = place("att2_hi", [P, 4, T], F32R, at=y_at)[0]
        O2l = place("att2_lo", [P, 4, T], F32R, at=y_at + K16 // 2)[0]
        ps = ctx.enter_context(nc.psum_tensor("ps", [P, 8, 512], F32))

        ident = C[:, CC["ident"]:CC["ident"] + P]
        ones_head = C[:, CC["ones_head"]:CC["ones_head"] + P]
        ones = C[:, CC["ones"]:CC["ones"] + P]

        consts_in, params_in, x_in, bias_in = (sem(n) for n in ("consts_in", "params_in", "x_in", "bias_in"))
        unit_in = [sem("unit_in_even"), sem("unit_in_odd")]
        hi_ready, lo_ready = sem("hi_ready"), sem("lo_ready")
        pair_full = sem("pair_full")
        half_done = sem("half_done")
        row_full = sem("row_full")
        row_taken = sem("row_taken")
        pair_taken = [sem("pair_taken_even"), sem("pair_taken_odd")]
        dve_order, act_order = sem("dve_order"), sem("act_order")
        rms_ready, xn_ready, ht_full, ht_hi, ht_lo = (
            sem(n) for n in ("rms_ready", "xn_ready", "ht_full", "ht_hi", "ht_lo"))
        rb_ready, rows_full, rows_ready, toe_stored, toe_skewed, toe_in = (
            sem(n) for n in ("rb_ready", "rows_full", "rows_ready", "toe_stored", "toe_skewed", "toe_in"))
        lora_pad, lora_raw_in, lora_shifted, lora_act = (
            sem(n) for n in ("lora_pad", "lora_raw_in", "lora_shifted", "lora_act"))
        lg_full, lg_read, nmx_ready, exp_ready, prob_ready, pt_full, pt_taken, pv_full, o_taken = (
            sem(n) for n in ("lg_full", "lg_read", "nmx_ready", "exp_ready", "prob_ready", "pt_full",
                             "pt_taken", "pv_full", "o_taken"))
        sink_in, ic_in, kd_in, x_back, gain_in, out_done = (
            sem(n) for n in ("sink_in", "ic_in", "kd_in", "x_back", "gain_in", "out_done"))
        gate_ready, merged_hi, merged_lo, split_hi, split_lo, x_ready, yrms_ready = (
            sem(n) for n in ("gate_ready", "merged_hi", "merged_lo", "split_hi", "split_lo", "x_ready", "yrms_ready"))
        hid_raw, hid_sq, hid_hi, hid_lo = (sem(n) for n in ("hid_raw", "hid_sq", "hid_hi", "hid_lo"))
        y_ready, z_ready, pd_ready, kraw_ready = (sem(n) for n in ("y_ready", "z_ready", "pd_ready", "kraw_ready"))
        lora_w_in = [sem("lora_w_in_even"), sem("lora_w_in_odd")]
        rkv_full = sem("rkv_full")
        rkv_taken = sem("rkv_taken")
        gate_tile = sem("gate_tile_ready")
        gate_stored = sem("gate_stored")
        gate_back = sem("gate_back")
        ident_r = sem("ident_r_ready")
        pair_open = sem("pair_open")
        rs = {n: sem(n) for n in ("z_full", "sig_ready", "zg_full", "g_ready", "sq_ready", "ss_full", "nrm_ready", "sqrt_ready",
                                  "rk_ready", "bonus_full", "csm_ready", "exps_ready", "rakb_ready",
                                  "tok_full", "tok_ready", "gram_full", "gram_taken", "m_ready", "x_full",
                                  "x1_ready", "tt_full", "t_ready", "t2_ready", "s_ready", "rhs_full", "rhs_ready",
                                  "sa_full", "sa_ready", "s_full", "y_full", "yraw_ready", "mu_full",
                                  "ysq_ready", "var_full", "std_ready", "u_full", "e_ready", "c_full", "tf_ready")}
        dve_rwkv = sem("dve_rwkv_order")

        class Order:

            def __init__(self, eng, s, base=0):
                self.eng, self.sem, self.base, self.n = eng, s, base, 0

            def __call__(self, ins):
                ins.then_inc(self.sem, 1)
                self.n += 1
                self.eng.wait_ge(self.sem, self.n + self.base)

        def f32(ap):
            return ap.bitcast(F32)

        def bank(b, n=512):
            return ps[:, b, 0:n]

        def pcol(name, k=0):
            c = PC[name] + k
            return PR[:, c:c + 1]

        def pcol_dyn(name, k):
            return PR[:, bass.ds(k + PC[name], 1)]

        items1 = []
        for hh in range(4):
            for qt in range(NT):
                segs, vals, off = [], [], 0
                for g in range(N_GROUPS):
                    nb = min(2, qt + 1) if g == 0 else qt + 1
                    h = g * 4 + hh
                    rows = slice(HD * (h % 2), HD * (h % 2) + HD)
                    k0 = (qt + 1 - nb) * P
                    segs.append(dict(bank=4 + g, n=nb * P, off=off,
                                     q=QK[rows, h // 2, qt * P:(qt + 1) * P],
                                     k=QK[rows, 6 + h // 2, k0:(qt + 1) * P],
                                     bias=TOE[:, hh * 3 + g, T - nb * P:T]))
                    off += nb * P
                    vals += [V1[:, kb, h * HD:(h + 1) * HD] for kb in range(qt + 1 - nb, qt + 1)]
                items1.append(dict(segs=segs, vals=vals, n=off, rows=slice(HD * (hh % 2), HD * (hh % 2) + HD),
                                   out=OAT[HD * (hh % 2):HD * (hh % 2) + HD, hh // 2, qt * P:(qt + 1) * P]))
        items2 = []
        for h in range(Q_HEADS2):
            for qt in range(NT):
                lo, hi = max(0, qt - 1), min(NT, qt + 2)
                rows = slice(HD * (h % 2), HD * (h % 2) + HD)
                kv = h // 4
                x0 = (lo - (qt - 1)) * P
                n = (hi - lo) * P
                items2.append(dict(
                    segs=[dict(bank=4 + len(items2) % 3, n=n, off=0, q=Q2[rows, h // 2, qt * P:(qt + 1) * P],
                               k=KD[rows, kv, lo * P:hi * P],
                               slope=-(2.0 ** -(h + 1)),
                               bias=C[:, CC["absdist"] + x0:CC["absdist"] + x0 + n])],
                    vals=[V2[:, kb, kv * HD:(kv + 1) * HD] for kb in range(lo, hi)], n=n, sink=h, rows=rows,
                    out=O2[rows, h // 2, qt * P:(qt + 1) * P]))
        att = [dict(items=items1, LG=LG1, PT=PT1, first=0), dict(items=items2, LG=LG2, PT=PT2, first=len(items1))]
        chunk = 0
        for a in att:
            for it in a["items"]:
                nv = len(it["vals"])
                it["chunks"] = [(c, min(4, nv - c)) for c in range(0, nv, 4)]
                it["chunk0"] = chunk
                chunk += len(it["chunks"])
                it["chunk1"] = chunk

        block = ctx.enter_context(nc.Block())

        @block.sync
        def _(sp):
            def load(n, slot):
                sp.dma_start(raw[:, slot, :], wpack[bass.ds(n, 1)].rearrange("a p f -> p (a f)")
                             if not isinstance(n, int) else wpack[n]).then_inc(unit_in[slot], 16)

            sp.dma_start(Xr[:], x.rearrange("(t p) d -> p t d", p=P)).then_inc(x_in, 16)
            sp.dma_start(C[:], ctab).then_inc(consts_in, 16)
            sp.dma_start(PR[:], params).then_inc(params_in, 16)
            sp.dma_start(RB[0:N_BUCKETS, :], rel_bias).then_inc(bias_in, 16)
            sp.dma_start(BT[:], btab).then_inc(bias_in, 16)
            load(0, 0)
            load(1, 1)
            with sp.Fori(1, N_UNITS // 2) as i:
                for slot in range(2):
                    sp.wait_ge(lo_ready, i * 2 + (slot - 1))
                    load(i * 2 + slot, slot)

        @block.gpsimd
        def _(pool):
            for n in range(N_UNITS):
                slot = n % 2
                pool.wait_ge(hi_ready, n + 1)
                nc.gpsimd.tensor_tensor(Wl[:, slot, :], raw[:, slot, :], f32(Wh[:, slot, :]),
                                        ALU.subtract).then_inc(lo_ready, 1)

        @block.tensor
        def _(pe):
            mm = nc.tensor.matmul

            def mm3(dst, wh, wl, ah, al, first, last):
                mm(dst, wh, ah, start=first, stop=False)
                mm(dst, wh, al, start=False, stop=False)
                return mm(dst, wl, ah, start=False, stop=last)

            def wait_pair(name, i, per, j, d):
                par = d % 2
                if isinstance(i, int):
                    if d + per * i >= 2:
                        pe.wait_ge(pair_taken[par], (d + per * i) // 2)
                else:
                    pe.wait_ge(pair_taken[par], i * (per // 2) + d // 2)

            def unit_cm(name, i, per, j, act=None, kts=KT, dper=None, dj=None):
                n, dper = UNIT0[name] + j, per if dper is None else dper
                d = USE0[name] + (j if dj is None else dj)
                ah, al = act or (HTh, HTl)
                cols = UNIT // kts
                slot = n % 2
                wh = Wh[:, slot, :].rearrange("p (k c) -> p k c", k=kts)
                wl = Wl[:, slot, :].rearrange("p (k c) -> p k c", k=kts)
                pe.wait_ge(lo_ready, i * per + (n + 1))
                for use in range(cols // 256):
                    wait_pair(name, i, dper, 0, d + use)
                    for c in range(2):
                        cc = use * 256 + c * P
                        for k in range(kts):
                            last = mm3(bank(2 * ((d + use) % 2) + c), wh[:, k, cc:cc + P], wl[:, k, cc:cc + P],
                                       ah[:, k, :], al[:, k, :], k == 0, k == kts - 1)
                    last.then_inc(pair_full, 1)

            def rows_of(slot, kts, k, c0, n):
                a = k * (UNIT // kts) + c0
                return Wh[:, slot, a:a + n], Wl[:, slot, a:a + n]

            def transposes(k):
                pe.wait_ge(xn_ready, NT * (k + 1))
                for kt in range(KT):
                    if k or kt >= 4:
                        pe.wait_ge(ht_lo, KT * k + kt - 3)
                    for tt in range(NT):
                        last = nc.tensor.transpose(ps[:, 4 + kt % 4, tt * P:(tt + 1) * P],
                                                   Y[:, tt, kt * P:(kt + 1) * P], ident)
                    last.then_inc(ht_full, 1)

            def attention(a):
                items, first, LG, PT = a["items"], a["first"], a["LG"], a["PT"]

                def logits(i):
                    if first + i:
                        pe.wait_ge(lg_read, first + i)
                    for s in items[i]["segs"]:
                        last = mm(bank(s["bank"], s["n"]), s["q"], s["k"], start=True, stop=True)
                    last.then_inc(lg_full, 1)

                logits(0)
                for i, it in enumerate(items):
                    if i + 1 < len(items):
                        logits(i + 1)
                    pe.wait_ge(prob_ready, first + i + 1)
                    for c, (v0, nv) in enumerate(it["chunks"]):
                        g = it["chunk0"] + c
                        if g >= 2:
                            pe.wait_ge(pt_taken, g - 1)
                        for j in range(nv):
                            last = nc.tensor.transpose(ps[:, 7 - 4 * (g % 2), j * P:(j + 1) * P],
                                                       LG[:, i % 2, (v0 + j) * P:(v0 + j + 1) * P], ident)
                        last.then_inc(pt_full, 1)
                    pe.wait_ge(pt_taken, it["chunk1"])
                    if first + i:
                        pe.wait_ge(o_taken, first + i)
                    for j, v in enumerate(it["vals"]):
                        last = mm(ps[it["rows"], 2, 0:P], v, PT[:, j, :], start=j == 0, stop=j == len(it["vals"]) - 1)
                    last.then_inc(pv_full, 1)

            def tok_major_out(name, k):
                for cb in range(2):
                    d = USE0[name] + 2 * cb
                    for half in range(2):
                        n = UNIT0[name] + 2 * cb + half
                        pe.wait_ge(lo_ready, n + 1)
                        for tt in range(NT):
                            use = d + tt // 2
                            if half == 0 and tt % 2 == 0:
                                wait_pair(name, 0, 0, 0, use)
                            for kk in range(4):
                                wh, wl = rows_of(n % 2, 4, kk, 0, 512)
                                kt = 4 * half + kk
                                tok = slice(tt * P, (tt + 1) * P)
                                last = mm3(bank(2 * (use % 2) + tt % 2), HTh[:, kt, tok], HTl[:, kt, tok],
                                           wh, wl, kt == 0, kt == KT - 1)
                            if half == 1 and tt % 2 == 1:
                                last.then_inc(pair_full, 1)
                        if half == 0:
                            last.then_inc(half_done, 1)

            def down(n_static, n_expr, g_static, rows_expr, hid_expr):
                pe.wait_ge(lo_ready, n_expr)
                pe.wait_ge(hid_lo, hid_expr)
                for tt in range(NT):
                    b = 4 + 2 * (tt % 2)
                    if rows_expr is not None or tt >= 2:
                        pe.wait_ge(row_taken, (rows_expr if rows_expr is not None else 0) + (tt - 1))
                    for k in range(2):
                        tok = slice(tt * P, (tt + 1) * P)
                        for c in range(2):
                            wh, wl = rows_of(n_static % 2, 2, k, c * 512, 512)
                            last = mm3(bank(b + c), HIh[:, g_static % 2, k, tok], HIl[:, g_static % 2, k, tok],
                                       wh, wl, k == 0, k == 1)
                    last.then_inc(row_full, 1)

            pe.wait_ge(bias_in, 32)
            pe.wait_ge(rb_ready, 1)
            for g in range(N_GROUPS):
                mm(ps[0:4, 4 + g, 0:T], RB[:, 4 * g:4 * g + 4], BT[:, g * TOE_LEN:g * TOE_LEN + T],
                   start=True, stop=True)
                last = mm(ps[0:4, 7, g * P:(g + 1) * P], RB[:, 4 * g:4 * g + 4],
                          BT[:, g * TOE_LEN + T:(g + 1) * TOE_LEN], start=True, stop=True)
            last.then_inc(rows_full, 1)

            pe.wait_ge(consts_in, 16)
            pe.wait_ge(rows_ready, 1)
            transposes(0)
            pe.wait_ge(ht_lo, KT)
            unit_cm("qk", 0, 2, 0)
            unit_cm("qk", 0, 2, 1)
            with pe.Fori(1, 3) as i:
                unit_cm("qk", i, 2, 0)
                unit_cm("qk", i, 2, 1)
            for u in range(3):
                n, d = UNIT0["v"] + u, USE0["v"] + u
                pe.wait_ge(lo_ready, n + 1)
                wait_pair("v", 0, 0, 0, d)
                for tt in range(NT):
                    for k in range(KT):
                        wh, wl = rows_of(n % 2, KT, k, 0, 256)
                        tok = slice(tt * P, (tt + 1) * P)
                        c0 = 256 * (tt % 2)
                        last = mm3(ps[:, 2 * (d % 2) + tt // 2, c0:c0 + 256], HTh[:, k, tok], HTl[:, k, tok],
                                   wh, wl, k == 0, k == KT - 1)
                last.then_inc(pair_full, 1)
            unit_cm("lora", 0, 0, 0)
            for par in range(2):
                pe.wait_ge(pair_taken[par], (USE0["rwkv"] + 1 - par) // 2)
            pe.wait_ge(toe_in, 16)
            attention(att[0])
            pe.wait_ge(o_taken, len(items1))

            nl = len(LEVELS)

            def pairwise(q, off):
                def w(name, m, k):
                    pe.wait_ge(rs[name], q * (2 * m) + (m * off + k))
                return w

            def inc(ins, name):
                ins.then_inc(rs[name], 1)

            def project(q, off, piece):
                u, c, k = piece // 16, piece % 16 // 8, piece % 8
                n = UNIT0["rwkv"] + 2 * off + u
                if piece % 16 == 0:
                    pe.wait_ge(lo_ready, q * 4 + (n + 1))
                    if not (isinstance(q, int) and 4 * q + 2 * off + u == 0):
                        pe.wait_ge(rkv_taken, q * 4 + (2 * off + u))
                wh, wl = rows_of(n % 2, KT, k, c * P, P)
                last = mm3(bank(c), wh, wl, HTh[:, k, :], HTl[:, k, :], k == 0, k == KT - 1)
                if piece % 16 == 15:
                    last.then_inc(rkv_full, 1)

            def prep(q, off, step):
                w, par = pairwise(q, off), off % 2
                if step == 0:
                    pe.wait_ge(lora_w_in[par], q * 32 + (32 * (off // 2) + 32))
                    pe.wait_ge(lora_act, 3)
                    if not (isinstance(q, int) and 2 * q + off == 0):
                        pe.wait_ge(pair_open, q * 2 + off)
                    mm(bank(2), LW[par][0:HD, 0, :], FWA[0:HD, 0, :], start=True, stop=True)
                    inc(mm(bank(3), LW[par][HD:P, 0, :], FWA[HD:P, 0, :], start=True, stop=True), "z_full")
                elif step == 1:
                    w("sig_ready", 1, 1)
                    inc(mm(bank(2), LW[par][:, 1, :], FWA[:, 1, :], start=True, stop=True), "zg_full")
                    w("sq_ready", 1, 1)
                    inc(mm(bank(3), ones_head, X2[:], start=True, stop=True), "ss_full")
                else:
                    w("rk_ready", 1, 1)
                    w("g_ready", 1, 1)
                    inc(mm(bank(2), ones_head, T1[:], start=True, stop=True), "bonus_full")

            def level_x(q, off, lv):
                w = pairwise(q, off)
                for h in range(2):
                    w("m_ready", 2 * nl, 2 * lv + h + 1)
                    if lv == 1:
                        w("t2_ready", 2, h + 1)
                    elif lv > 1:
                        w("t_ready", 2 * (nl - 1), 2 * (lv - 2) + h + 1)
                    for t in range(NT):
                        last = mm(ps[:, 4 + h, t * P:(t + 1) * P], Mb[h][:, t, :],
                                  Tb[h][:, t, :] if lv else identR[:], start=True, stop=True)
                    inc(last, "x_full")

            def level_t(q, off, lv):
                w = pairwise(q, off)
                for h in range(2):
                    w("x1_ready", 2 * (nl - 1), 2 * (lv - 1) + h + 1)
                    for t in range(NT):
                        mm(ps[:, 6 + h, t * P:(t + 1) * P], Xb[h][:, t, :], TT[h][:, t, :], start=True, stop=True)
                    for t in range(NT):
                        last = mm(ps[:, 4 + h, t * P:(t + 1) * P], TT[h][:, t, :], Xb[h][:, t, :],
                                  start=True, stop=True)
                    inc(last, "tt_full")

            def refine_u(q, off):
                w = pairwise(q, off)
                for h in range(2):
                    w("t_ready", 2 * (nl - 1), 2 * (nl - 2) + h + 1)
                    for t in range(NT):
                        dst = ps[:, 4 + h, t * P:(t + 1) * P]
                        mm(dst, GM[h][:, t, 3, :], f32(Tb[h][:, t, :]), start=True, stop=False)
                        last = mm(dst, identR[:], identR[:], start=False, stop=True)
                    inc(last, "u_full")

            def refine_c(q, off):
                w = pairwise(q, off)
                for h in range(2):
                    w("e_ready", 2, h + 1)
                    for t in range(NT):
                        last = mm(ps[:, 6 + h, t * P:(t + 1) * P], Xb[h][:, t, :], TT[h][:, t, :],
                                  start=True, stop=True)
                    inc(last, "c_full")

            def chunks(q, off, fill):
                w, ra = pairwise(q, off), RA[off % 2]
                heads = [slice(HD * h, HD * h + HD) for h in range(2)]
                w("tf_ready", 2, 2)
                for t in range(NT):
                    tok = slice(t * P, (t + 1) * P)
                    w("s_ready", NT, t + 1)
                    for h, hc in enumerate(heads):
                        mm(bank(4 + h, HD), ra[hc, t, 1, :], S[hc, :], start=True, stop=False)
                        last = mm(bank(4 + h, HD), GM[h][:, t, 1, :], TV[:, t, hc], start=False, stop=True)
                    inc(last, "rhs_full")
                    for h, hc in enumerate(heads):
                        mm(ps[hc, 6, tok], S[hc, :], ra[hc, t, 0, :], start=True, stop=False)
                    w("rhs_ready", NT, t + 1)
                    for h, hc in enumerate(heads):
                        last = mm(ps[:, 4, P + HD * h:P + HD * h + HD], TF[h][:, t, :], RH[:, hc], start=True, stop=True)
                    inc(last, "sa_full")
                    fill(1)
                    w("sa_ready", NT, t + 1)
                    if t < NT - 1:
                        for h, hc in enumerate(heads):
                            mm(ps[hc, 5, P:P + HD], TB[:, t, hc], SA[:, hc], start=True, stop=False)
                            last = mm(ps[hc, 5, P:P + HD], TK[:, t, hc], TV[:, t, hc], start=False, stop=True)
                        inc(last, "s_full")
                    for h, hc in enumerate(heads):
                        mm(ps[hc, 6, tok], TV[:, t, hc], GM[h][:, t, 0, :], start=False, stop=False)
                        last = mm(ps[hc, 6, tok], SA[:, hc], GM[h][:, t, 2, :], start=False, stop=True)
                    if t < NT - 1:
                        fill(1)
                inc(last, "y_full")
                fill(1)

            def norm_mean(q, off):
                w = pairwise(q, off)
                w("yraw_ready", 1, 1)
                inc(mm(bank(2), ones_head, E[:], start=True, stop=True), "mu_full")

            def norm_var(q, off):
                w = pairwise(q, off)
                w("ysq_ready", 1, 1)
                inc(mm(bank(3), ones_head, X2[:], start=True, stop=True), "var_full")

            def to_tokens(q, off):
                w = pairwise(q, off)
                w("rakb_ready", 1, 1)
                for b, src in ((5, RAW[:, off % 2, 2, 1:T + 1]), (6, KB[:, 0, :]), (7, KB[:, 1, :])):
                    for t in range(NT):
                        last = nc.tensor.transpose(ps[:, b, t * P:(t + 1) * P], src[:, t * P:(t + 1) * P], ident)
                    inc(last, "tok_full")

            def grams(q, off):
                w = pairwise(q, off)
                w("tok_ready", 3, 3)
                for t in range(NT):
                    if t >= 2:
                        w("gram_taken", NT, t - 1)
                    for h in range(2):
                        rows = slice(HD * h, HD * h + HD)
                        b = 4 + 2 * (t % 2) + h
                        ra = RA[off % 2][rows, t, :, :].rearrange("p a b -> p (a b)")
                        mm(ps[:, b, 0:256], KB[rows, 0, t * P:(t + 1) * P], ra, start=True, stop=True)
                        last = mm(ps[:, b, 256:512], KB[rows, 1, t * P:(t + 1) * P], ra, start=True, stop=True)
                    inc(last, "gram_full")

            def first_levels(q, off, fill, norm):
                level_x(q, off, 0)
                if norm:
                    norm_mean(q, off - 1)
                fill(2)
                level_x(q, off, 1)
                if norm:
                    norm_var(q, off - 1)
                fill(2)
                level_t(q, off, 1)
                fill(2)

            def pair_step(q, off, ahead, project_ahead):
                pieces = iter(range(32)) if project_ahead else iter(())

                def fill(n):
                    for _ in range(n):
                        for piece in pieces:
                            project(q, off + 2, piece)
                            break

                for lv in range(2, nl):
                    level_x(q, off, lv)
                    fill(2)
                    level_t(q, off, lv)
                    if 3 <= lv < 6:
                        if ahead:
                            prep(q, off + 1, lv - 3)
                    else:
                        fill(2)
                refine_u(q, off)
                fill(2)
                refine_c(q, off)
                chunks(q, off, fill)
                if ahead:
                    fill(2)
                    pairwise(q, off)("yraw_ready", 1, 1)
                    to_tokens(q, off + 1)
                    grams(q, off + 1)
                    first_levels(q, off + 1, fill, True)
                    assert not list(pieces)
                else:
                    norm_mean(q, off)
                    norm_var(q, off)

            for off in range(2):
                for piece in range(32):
                    project(0, off, piece)
            for step in range(3):
                prep(0, 0, step)
            pe.wait_ge(ident_r, 1)
            to_tokens(0, 0)
            grams(0, 0)
            first_levels(0, 0, lambda n: None, False)
            with pe.Fori(0, PAIRS // 2 - 1) as q:
                pair_step(q, 0, True, True)
                pair_step(q, 1, True, True)
            pair_step(PAIRS // 2 - 1, 0, True, False)
            pair_step(PAIRS // 2 - 1, 1, False, False)

            unit_cm("gate0", 0, 2, 0)
            pe.wait_ge(pair_open, PAIRS + 1)
            unit_cm("gate0", 0, 2, 1)
            unit_cm("gate0", 1, 2, 0)
            unit_cm("gate0", 1, 2, 1)
            pe.wait_ge(split_lo, 1)
            unit_cm("attb", 0, 0, 0, act=(OAh, OAl), kts=2)
            pe.wait_ge(split_lo, 2)
            for i in range(2):
                unit_cm("rwkvb", i, 2, 0, act=(ORh, ORl))
                unit_cm("rwkvb", i, 2, 1, act=(ORh, ORl))
            pe.wait_ge(merged_lo, 1)
            tok_major_out("wout", 0)
            transposes(1)
            pe.wait_ge(ht_lo, 2 * KT)
            n0 = UNIT0["ffn"]
            unit_cm("ffn", 0, 0, 0)

            def up1(i, per, j, k):
                n = n0 + k
                pe.wait_ge(lo_ready, i * 4 + (n + 1))
                d = USE0["ffn"] + j
                wait_pair("ffn", i, 2, 0, d)
                for c in range(2):
                    for kt in range(KT):
                        wh, wl = rows_of(n % 2, KT, kt, c * P, P)
                        last = mm3(bank(2 * (d % 2) + c), wh, wl, HTh[:, kt, :], HTl[:, kt, :], kt == 0, kt == KT - 1)
                last.then_inc(pair_full, 1)

            def ffn1_step(i, rows):
                up1(i, 2, 1, 1)
                down(n0 + 2, i * 4 + (n0 + 3), 0, rows(0), i * 2 + 1)
                up1(i, 2, 2, 3)
                down(n0 + 4, i * 4 + (n0 + 5), 1, rows(1), i * 2 + 2)

            ffn1_step(0, lambda s: None if s == 0 else NT)
            with pe.Fori(1, FF1_GROUPS // 2 - 1) as i:
                ffn1_step(i, lambda s: i * (2 * NT) + NT * s)
            i = FF1_GROUPS // 2 - 1
            up1(i, 2, 1, 1)
            down(n0 + 2, 4 * i + n0 + 3, 0, 2 * NT * i, 2 * i + 1)
            down(n0 + 3, 4 * i + n0 + 4, 1, 2 * NT * i + NT, 2 * i + 2)

            transposes(2)
            pe.wait_ge(ht_lo, 3 * KT)
            for u in range(2):
                unit_cm("pool", 0, 0, u)
            for u in range(2):
                unit_cm("q2", 0, 0, u)
            n, d = UNIT0["kv2"], USE0["kv2"]
            pe.wait_ge(lo_ready, n + 1)
            wait_pair("kv2", 0, 0, 0, d)
            for k in range(KT):
                wh, wl = rows_of(n % 2, KT, k, 0, P)
                mm3(bank(2 * (d % 2)), wh, wl, HTh[:, k, :], HTl[:, k, :], k == 0, k == KT - 1)
            for tt in range(NT):
                tok = slice(tt * P, (tt + 1) * P)
                for k in range(KT):
                    wh, wl = rows_of(n % 2, KT, k, P, P)
                    last = mm3(ps[:, 2 * (d % 2) + 1, tok], HTh[:, k, tok], HTl[:, k, tok], wh, wl,
                               k == 0, k == KT - 1)
            last.then_inc(pair_full, 1)
            pe.wait_ge(pd_ready, 4)
            n, d = UNIT0["group"], USE0["group"]
            pe.wait_ge(lo_ready, n + 1)
            for use in range(2):
                wait_pair("group", 0, 0, 0, d + use)
                for c in range(2):
                    g = 2 * use + c
                    wh, wl = Wh[:, n % 2, g * P:(g + 1) * P], Wl[:, n % 2, g * P:(g + 1) * P]
                    last = mm3(bank(2 * ((d + use) % 2) + c), wh, wl, PDh[:, g, :], PDl[:, g, :], True, True)
                last.then_inc(pair_full, 1)
            for par in range(2):
                pe.wait_ge(pair_taken[par], (USE0["gatep"] + 1 - par) // 2)
            pe.wait_ge(kd_in, 32)
            attention(att[1])
            pe.wait_ge(o_taken, len(items1) + len(items2))
            for name in ("gatep", "gatea"):
                for i in range(2):
                    unit_cm(name, i, 2, 0)
                    unit_cm(name, i, 2, 1)
            for u in range(2):
                unit_cm("poolb", 0, 0, u, act=(YPh, YPl), kts=4, dj=2 * u)
            pe.wait_ge(split_lo, 3)
            for u in range(2):
                unit_cm("attnb", 0, 0, u, act=(O2h, O2l), kts=4, dj=2 * u)
            pe.wait_ge(merged_lo, 2)
            tok_major_out("wout2", 1)
            transposes(3)
            pe.wait_ge(ht_lo, 4 * KT)
            m0 = UNIT0["ffn2"]
            R0, H0 = NT * FF1_GROUPS, FF1_GROUPS

            def up2(i, j, k):
                for v in range(2):
                    n = m0 + k + v
                    pe.wait_ge(lo_ready, i * 6 + (n + 1))
                    d = USE0["ffn2"] + 2 * j + v
                    wait_pair("ffn2", i, 4, 0, d)
                    for c in range(2):
                        for kt in range(KT):
                            wh, wl = rows_of(n % 2, KT, kt, c * P, P)
                            last = mm3(bank(2 * (d % 2) + c), wh, wl, HTh[:, kt, :], HTl[:, kt, :],
                                       kt == 0, kt == KT - 1)
                    last.then_inc(pair_full, 1)

            up2(0, 0, 0)
            with pe.Fori(0, FF2_GROUPS // 2) as i:
                up2(i, 1, 2)
                down(m0 + 4, i * 6 + (m0 + 5), 0, i * (2 * NT) + R0, i * 2 + (H0 + 1))
                up2(i, 2, 5)
                down(m0 + 7, i * 6 + (m0 + 8), 1, i * (2 * NT) + (R0 + NT), i * 2 + (H0 + 2))
            i = FF2_GROUPS // 2
            down(m0 + 2 + 6 * i, m0 + 6 * i + 3, 0, R0 + 2 * NT * i, H0 + 2 * i + 1)

        @block.scalar
        def _(act):
            order = Order(act, act_order)
            actf = nc.scalar.activation

            def square_sums(src, k, ready, count):
                for tt in range(NT):
                    order(actf(JUNK[:], src[:, tt, :], ACT.Square, accum_out=stat[:, tt:tt + 1]))
                actf(stat[:, 4:8], stat[:, 0:4], ACT.Sqrt, scale=1.0 / D,
                     bias=C[:, CC["eps"]:CC["eps"] + 1]).then_inc(ready, 1)

            def split_transposed(k, gain):
                for kt in range(KT):
                    act.wait_ge(ht_full, KT * k + kt + 1)
                    actf(HTh[:, kt, :], bank(4 + kt % 4), ACT.Copy, scale=pcol(gain, kt)).then_inc(ht_hi, 1)

            def hi(n, i=0, per=0):
                act.wait_ge(unit_in[n % 2], i * (8 * per) + 16 * (n // 2 + 1))
                actf(Wh[:, n % 2, :], raw[:, n % 2, :], ACT.Copy).then_inc(hi_ready, 1)

            def evac_cols(name, i, per, j, dst, func=ACT.Copy, bias=None, scale=1.0, dst_per=2):
                d = USE0[name] + j
                act.wait_ge(pair_full, i * per + (d + 1))
                hi(UNIT0[name] + j + 2, i, per)
                b = 2 * (d % 2)
                if bias is None:
                    last = actf(dst, ps[:, b:b + 2, :], func, scale=scale)
                else:
                    for c in range(2):
                        last = actf(dst[:, c, :], bank(b + c), func, bias=bias(c))
                last.then_inc(pair_taken[d % 2], 1)

            def attention(a):
                items, first, LG, PT = a["items"], a["first"], a["LG"], a["PT"]
                for i, it in enumerate(items):
                    act.wait_ge(nmx_ready, first + i + 1)
                    st = 16 + 8 * (i % 2)
                    if "sink" in it:
                        order(actf(stat[:, st + 3:st + 4], SNK[:, it["sink"]:it["sink"] + 1], ACT.Exp,
                                   bias=stat[:, st + 1:st + 2]))
                    actf(LG[:, i % 2, 0:it["n"]], LG[:, i % 2, 0:it["n"]], ACT.Exp, bias=stat[:, st + 1:st + 2],
                         accum_out=stat[:, st + 2:st + 3]).then_inc(exp_ready, 1)
                    for c, (v0, nv) in enumerate(it["chunks"]):
                        g = it["chunk0"] + c
                        act.wait_ge(pt_full, g + 1)
                        if c == 0 and first + i:
                            act.wait_ge(pv_full, first + i)
                        actf(PT[:, v0:v0 + nv, :].rearrange("p a b -> p (a b)"), bank(7 - 4 * (g % 2), nv * P),
                             ACT.Copy).then_inc(pt_taken, 1)
                    act.wait_ge(pv_full, first + i + 1)
                    actf(it["out"], ps[it["rows"], 2, 0:P], ACT.Copy).then_inc(o_taken, 1)

            hi(0)
            hi(1)
            act.wait_ge(rows_full, 1)
            order(actf(RROW[:, :, 0:T], ps[0:4, 4:7, :], ACT.Copy))
            actf(RROW[:, :, T:TOE_LEN], ps[0:4, 7, 0:3 * P].rearrange("h (g c) -> h g c", g=3),
                 ACT.Copy).then_inc(rows_ready, 1)
            act.wait_ge(rows_ready, 1)
            act.dma_start(toe_dram, RROW[:]).then_inc(toe_stored, 16)
            act.wait_ge(toe_stored, 16)
            act.dma_start(bass.AP(toe_skew.tensor, 0, [[TOE_LEN + 1, P], [SKEW, 12], [1, TOE_LEN]]),
                          bass.AP(toe_dram.tensor, 0, [[0, P], [TOE_LEN, 12], [1, TOE_LEN]])).then_inc(toe_skewed, 16)
            act.wait_ge(toe_skewed, 16)
            act.dma_start(TOE[:], bass.AP(toe_skew.tensor, P - 1, [[TOE_LEN, P], [SKEW, 12], [1, T]])
                          ).then_inc(toe_in, 16)

            act.wait_ge(x_in, 16)
            act.wait_ge(consts_in, 16)
            act.wait_ge(params_in, 16)
            square_sums(Xr, 0, rms_ready, 1)
            split_transposed(0, "mix_pre")
            evac_cols("qk", 0, 2, 0, QK[:, 0:2, :])
            evac_cols("qk", 0, 2, 1, QK[:, 2:4, :])
            with act.Fori(1, 3) as i:
                evac_cols("qk", i, 2, 0, QK[:, bass.ds(i * 4, 2), :])
                evac_cols("qk", i, 2, 1, QK[:, bass.ds(i * 4 + 2, 2), :])
            for u in range(3):
                d = USE0["v"] + u
                act.wait_ge(pair_full, d + 1)
                hi(UNIT0["v"] + u + 2)
                actf(V1[:, :, 256 * u:256 * u + 256],
                     ps[:, 2 * (d % 2):2 * (d % 2) + 2, :].rearrange("p a (b c) -> p (a b) c", b=2),
                     ACT.Copy).then_inc(pair_taken[d % 2], 1)
            d = USE0["lora"]
            act.wait_ge(pair_full, d + 1)
            hi(UNIT0["lora"] + 2)
            actf(LRAW[:, :, 1:T + 1], ps[:, 2 * (d % 2):2 * (d % 2) + 2, :], ACT.Copy
                 ).then_inc(pair_taken[d % 2], 1)
            act.wait_ge(lora_shifted, 1)
            actf(FWA[0:HD, 0, :], LTMP[0:HD, 0, :], ACT.Tanh).then_inc(lora_act, 1)
            actf(FWA[HD:P, 0, :], LTMP[HD:P, 0, :], ACT.Copy).then_inc(lora_act, 1)
            actf(FWA[:, 1, :], LTMP[:, 1, :], ACT.Sigmoid).then_inc(lora_act, 1)
            attention(att[0])

            nl = len(LEVELS)

            def pairwise(q, off):
                def w(name, m, k):
                    act.wait_ge(rs[name], q * (2 * m) + (m * off + k))
                return w

            def inc(ins, name):
                ins.then_inc(rs[name], 1)

            def col(name, q, off):
                return pcol_dyn(name, q * 2 + off) if not isinstance(q, int) else pcol(name, q * 2 + off)

            def lora_weights(q, off):
                c = q * 256 + off * P
                c = slice(c, c + P) if isinstance(q, int) else bass.ds(c, P)
                act.dma_start(LW[off % 2][:, 0, :], lora_wa[:, c]).then_inc(lora_w_in[off % 2], 16)
                act.dma_start(LW[off % 2][:, 1, :], lora_g[:, c]).then_inc(lora_w_in[off % 2], 16)

            def take_rk(q, off):
                act.wait_ge(rkv_full, q * 4 + (2 * off + 1))
                actf(RAW[:, off % 2, 0:2, 1:T + 1], ps[:, 0:2, :], ACT.Copy).then_inc(rkv_taken, 1)
                hi(UNIT0["rwkv"] + 2 * off + 2, q, 4)

            def take_vg(q, off):
                act.wait_ge(rkv_full, q * 4 + (2 * off + 2))
                hi(UNIT0["rwkv"] + 2 * off + 3, q, 4)
                if not (isinstance(q, int) and 2 * q + off == 0):
                    act.wait_ge(gate_stored, q * 32 + 16 * off)
                actf(GT[:], bank(1), ACT.Sigmoid, bias=col("b_gate", q, off + KT)).then_inc(gate_tile, 1)
                actf(RAW[:, off % 2, 2, 1:T + 1], bank(0), ACT.Copy).then_inc(rkv_taken, 1)
                act.wait_ge(gate_tile, q * 2 + (off + 1))
                dst = gate1_dram[q * 2 + off] if isinstance(q, int) else \
                    gate1_dram[bass.ds(q * 2 + off, 1)].rearrange("a p t -> p (a t)")
                act.dma_start(dst, GT[:]).then_inc(gate_stored, 16)

            def prep(q, off, step):
                w, par = pairwise(q, off), off % 2
                if step == 0:
                    w("z_full", 1, 1)
                    actf(SZ[:], bank(2), ACT.Sigmoid, bias=col("w0", q, off))
                    inc(actf(Ab[:], bank(3), ACT.Sigmoid, bias=col("a0", q, off)), "sig_ready")
                elif step == 1:
                    w("zg_full", 1, 1)
                    inc(actf(Gb[par][:], bank(2), ACT.Copy), "g_ready")
                elif step == 2:
                    w("nrm_ready", 1, 1)
                    inc(actf(E[:], E[:], ACT.Sqrt), "sqrt_ready")
                else:
                    w("csm_ready", 1, 1)
                    actf(LM[:, par, 0, :], CS[:].rearrange("p (t c) -> p t c", c=P)[:, :, HD - 1], ACT.Exp,
                         scale=-KAPPA)
                    actf(X2[:], E[:], ACT.Exp, scale=KAPPA)
                    actf(E[:], E[:], ACT.Exp, scale=-KAPPA)
                    inc(actf(T1[:], T1[:], ACT.Exp, scale=-KAPPA), "exps_ready")

            def level(q, off, lv):
                w = pairwise(q, off)
                for h in range(2):
                    w("tt_full", 2 * (nl - 1), 2 * (lv - 1) + h + 1)
                    actf(TT[h][:].rearrange("p a b -> p (a b)"), bank(6 + h), ACT.Copy)
                    inc(actf(Tb[h][:].rearrange("p a b -> p (a b)"), bank(4 + h), ACT.Copy), "t_ready")

            def chunks(q, off, ahead):
                w = pairwise(q, off)
                for t in range(NT):
                    w("rhs_full", NT, t + 1)
                    inc(actf(RH[:].rearrange("p (h c) -> p h c", h=2), ps[:, 4:6, 0:HD], ACT.Copy), "rhs_ready")
                    if ahead and t == 0:
                        prep(q, off + 1, 3)

            def norm_in(q, off, ahead):
                w = pairwise(q, off)
                w("y_full", 1, 1)
                if ahead:
                    pairwise(q, off + 1)("rakb_ready", 1, 1)
                inc(actf(E[:], bank(6), ACT.Copy), "yraw_ready")

            def norm_std(q, off):
                w = pairwise(q, off)
                w("var_full", 1, 1)
                inc(actf(X2[:], bank(3), ACT.Sqrt, scale=1.0 / HD, bias=C[:, CC["ln_eps"]:CC["ln_eps"] + 1]),
                    "std_ready")

            def to_tokens(q, off):
                w = pairwise(q, off)
                for k, (b, dst) in enumerate(((5, TV), (6, TK), (7, TB))):
                    w("tok_full", 3, k + 1)
                    inc(actf(dst[:].rearrange("p a b -> p (a b)"), bank(b), ACT.Copy), "tok_ready")

            def pair_step(q, off, ahead, project_ahead):
                if project_ahead:
                    lora_weights(q, off + 2)
                for lv in range(2, nl):
                    level(q, off, lv)
                    if ahead and 3 <= lv < 6:
                        prep(q, off + 1, lv - 3)
                if project_ahead:
                    take_rk(q, off + 2)
                chunks(q, off, ahead)
                norm_in(q, off, ahead)
                if ahead:
                    to_tokens(q, off + 1)
                norm_std(q, off)
                if ahead:
                    level(q, off + 1, 1)
                if project_ahead:
                    take_vg(q, off + 2)

            act.wait_ge(pair_open, 1)
            actf(identR[:], ident, ACT.Copy).then_inc(ident_r, 1)
            for off in range(2):
                lora_weights(0, off)
                take_rk(0, off)
                take_vg(0, off)
            for step in range(4):
                prep(0, 0, step)
            to_tokens(0, 0)
            level(0, 0, 1)
            with act.Fori(0, PAIRS // 2 - 1) as q:
                pair_step(q, 0, True, True)
                pair_step(q, 1, True, True)
            pair_step(PAIRS // 2 - 1, 0, True, False)
            pair_step(PAIRS // 2 - 1, 1, False, False)

            act.wait_ge(pair_open, PAIRS + 1)
            actf(OAh[:], OAT[:], ACT.Copy).then_inc(split_hi, 1)
            actf(ORh[:], ORW[:], ACT.Copy).then_inc(split_hi, 1)
            for u in range(4):
                evac_cols("gate0", 0, 0, u, MG[:, 2 * u:2 * u + 2, :], ACT.Sigmoid,
                          bias=lambda c, u=u: pcol("b_gate", 2 * u + c))
            act.dma_start(GN[:], post_gains[0]).then_inc(gain_in, 16)
            act.wait_ge(gate_stored, 16 * PAIRS)
            act.dma_start(G1[:], gate1_dram.rearrange("k p t -> p k t")).then_inc(gate_back, 16)
            act.wait_ge(pair_full, USE0["attb"] + 4)
            hi(UNIT0["attb"] + 2)
            act.wait_ge(split_lo, 2)
            act.dma_start(Xr[:], x.rearrange("(t p) d -> p t d", p=P)).then_inc(x_back, 16)

            for u in range(4):
                act.wait_ge(pair_full, USE0["rwkvb"] + u + 1)
                hi(UNIT0["rwkvb"] + u + 2)

            def merged_and_out(k, name, M):
                act.wait_ge(merged_hi, 2 * k + 1)
                actf(HTh[:], M[:], ACT.Copy).then_inc(merged_hi, 1)
                for u in range(4):
                    d = USE0[name] + u
                    if u % 2 == 0:
                        act.wait_ge(half_done, 2 * k + u // 2 + 1)
                        hi(UNIT0[name] + u + 2)
                    act.wait_ge(pair_full, d + 1)
                    if u % 2 == 1:
                        hi(UNIT0[name] + u + 2)
                    tt = 2 * (u % 2)
                    actf(Y[:, tt:tt + 2, 512 * (u // 2):512 * (u // 2) + 512], ps[:, 2 * (d % 2):2 * (d % 2) + 2, :],
                         ACT.Copy).then_inc(pair_taken[d % 2], 1)

            merged_and_out(0, "wout", MG)
            for d in (USE0["wout"] + 2, USE0["wout"] + 3):
                act.wait_ge(pair_taken[d % 2], d // 2 + 1)
            square_sums(Y, 0, yrms_ready, 1)
            act.wait_ge(x_ready, 1)
            square_sums(Xr, 1, rms_ready, 2)
            act.dma_start(GN[:], post_gains[1]).then_inc(gain_in, 16)
            split_transposed(1, "ffn_pre")

            def hidden1(i, j):
                d = USE0["ffn"] + j
                n = UNIT0["ffn"] + 2 * j
                if not (isinstance(i, int) and i == 0):
                    act.wait_ge(row_full, i * (2 * NT) + (NT * (j - 1)))
                    hi(n, i, 4)
                act.wait_ge(pair_full, i * 2 + (d + 1))
                hi(n + 2 if isinstance(i, int) and i == 0 and j == 0 else n + 1, i, 4)
                b = 2 * (d % 2)
                if not (isinstance(i, int) and i == 0 and j == 0):
                    act.wait_ge(hid_sq, i * 2 + j)
                actf(HR[:], ps[:, b:b + 2, :], ACT.Relu).then_inc(pair_taken[d % 2], 1)
                act.wait_ge(hid_sq, i * 2 + (j + 1))
                actf(HIh[:, j % 2, :, :], HR2[:], ACT.Copy).then_inc(hid_hi, 1)

            hidden1(0, 0)
            hidden1(0, 1)
            with act.Fori(1, FF1_GROUPS // 2) as i:
                hidden1(i, 0)
                hidden1(i, 1)
            for g in (FF1_GROUPS - 1, FF1_GROUPS):
                act.wait_ge(row_full, NT * g)
                hi(UNIT0["ffn"] + FF1_GROUPS + g + 1)
            act.wait_ge(row_taken, NT * FF1_GROUPS)
            square_sums(Y, 0, yrms_ready, 2)
            act.wait_ge(x_ready, 2)
            square_sums(Xr, 2, rms_ready, 3)
            split_transposed(2, "mix2")

            act.dma_start(SNK[:], sink).then_inc(sink_in, 16)
            act.dma_start(IC[:].rearrange("p w t -> p (w t)"), icount).then_inc(ic_in, 16)
            act.wait_ge(kraw_ready, 1)
            for u in range(2):
                evac_cols("pool", 0, 0, u, Zp[:, 2 * u:2 * u + 2, 16:16 + T])
            for u in range(2):
                evac_cols("q2", 0, 0, u, Q2[:, 2 * u:2 * u + 2, :], scale=HD ** -0.5)
            d = USE0["kv2"]
            act.wait_ge(pair_full, d + 1)
            hi(UNIT0["kv2"] + 2)
            b = 2 * (d % 2)
            order(actf(KD[0:HD, 0, :], ps[0:HD, b, :], ACT.Copy))
            order(actf(KD[HD:P, 1, :], ps[HD:P, b, :], ACT.Copy))
            act.dma_start(KD[HD:P, 0, :], KD[0:HD, 0, :]).then_inc(kd_in, 16)
            act.dma_start(KD[0:HD, 1, :], KD[HD:P, 1, :]).then_inc(kd_in, 16)
            actf(V2[:].rearrange("p a b -> p (a b)"), bank(b + 1), ACT.Copy).then_inc(pair_taken[d % 2], 1)
            for u in range(2):
                d = USE0["group"] + u
                act.wait_ge(pair_full, d + 1)
                for c in range(2):
                    g = 2 * u + c
                    last = actf(YPh[:, g, :], bank(2 * (d % 2) + c), ACT.Copy, scale=pcol("pool_scale", g))
                last.then_inc(split_hi, 1)
            hi(UNIT0["group"] + 2)
            act.wait_ge(sink_in, 16)
            attention(att[1])
            for u in range(4):
                evac_cols("gatep", 0, 0, u, MG2[:, 2 * u:2 * u + 2, :], ACT.Sigmoid)
            for u in range(4):
                evac_cols("gatea", 0, 0, u, G2[:, 2 * u:2 * u + 2, :], ACT.Sigmoid)
            actf(O2h[:], O2[:], ACT.Copy).then_inc(split_hi, 1)
            for name in ("poolb", "attnb"):
                for u in range(2):
                    act.wait_ge(pair_full, USE0[name] + 2 * u + 2)
                    hi(UNIT0[name] + u + 2)
            merged_and_out(1, "wout2", MG2)
            act.wait_ge(x_ready, 3)
            square_sums(Xr, 3, rms_ready, 4)
            act.dma_start(GN[:], post_gains[2]).then_inc(gain_in, 16)
            split_transposed(3, "ffn2")

            def hidden2(i, j):
                d = USE0["ffn2"] + 2 * j
                n = UNIT0["ffn2"] + 3 * j
                g_first = isinstance(i, int) and i == 0
                act.wait_ge(row_full, i * (2 * NT) + (NT * (FF1_GROUPS + j - 1)))
                if not g_first:
                    hi(n, i, 6)
                act.wait_ge(pair_full, i * 4 + (d + 1))
                hi(n + 2 if g_first and j == 0 else n + 1, i, 6)
                b = 2 * (d % 2)
                act.wait_ge(hid_sq, i * 2 + (FF1_GROUPS + j))
                actf(HR[:], ps[:, b:b + 2, :], ACT.Sigmoid).then_inc(hid_raw, 1)
                act.wait_ge(pair_full, i * 4 + (d + 2))
                hi(n + 3 if g_first and j == 0 else n + 2, i, 6)
                act.wait_ge(hid_sq, i * 2 + (FF1_GROUPS + j + 1))
                actf(HIh[:, j % 2, :, :], HR2[:], ACT.Copy).then_inc(hid_hi, 1)

            hidden2(0, 0)
            hidden2(0, 1)
            with act.Fori(1, FF2_GROUPS // 2) as i:
                hidden2(i, 0)
                hidden2(i, 1)
            hidden2(FF2_GROUPS // 2, 0)
            act.wait_ge(x_ready, 4)
            square_sums(Xr, 4, rms_ready, 5)
            act.wait_ge(y_ready, 1)
            act.dma_start(out.rearrange("(t p) d -> p t d", p=P), Y[:]).then_inc(out_done, 16)
            act.wait_ge(out_done, 16)

        @block.vector
        def _(dve):
            order = Order(dve, dve_order)
            v = nc.vector

            def used(d):
                dve.wait_ge(pair_taken[d % 2], d // 2 + 1)

            def normalise(k):
                dve.wait_ge(rms_ready, k + 1)
                order(v.reciprocal(stat[:, 8:12], stat[:, 4:8]))
                for tt in range(NT):
                    v.tensor_scalar(Y[:, tt, :], Xr[:, tt, :], stat[:, 8 + tt:9 + tt], None,
                                    ALU.mult).then_inc(xn_ready, 1)

            def split_transposed(k, gain):
                for kt in range(KT):
                    dve.wait_ge(ht_hi, KT * k + kt + 1)
                    v.scalar_tensor_tensor(HTl[:, kt, :], bank(4 + kt % 4), pcol(gain, kt), f32(HTh[:, kt, :]),
                                           ALU.mult, ALU.subtract).then_inc(ht_lo, 1)

            def add_normed(k):
                dve.wait_ge(yrms_ready, k + 1)
                dve.wait_ge(gain_in, 16 * (k + 1))
                order(v.reciprocal(stat[:, 8:12], stat[:, 4:8]))
                for tt in range(NT):
                    order(v.scalar_tensor_tensor(Y[:, tt, :], Y[:, tt, :], stat[:, 8 + tt:9 + tt], GN[:],
                                                 ALU.mult, ALU.mult))
                v.tensor_tensor(Xr[:], Xr[:], Y[:], ALU.add).then_inc(x_ready, 1)
                dve.wait_ge(x_ready, [1, 2][k])

            def attention(a):
                items, first, LG = a["items"], a["first"], a["LG"]
                for i, it in enumerate(items):
                    st = 16 + 8 * (i % 2)
                    mx, nmx, total, es, rec = (stat[:, st + c:st + c + 1] for c in range(5))
                    dve.wait_ge(lg_full, first + i + 1)
                    if i >= 2:
                        dve.wait_ge(pt_full, items[i - 2]["chunk1"])
                    for s in it["segs"]:
                        dst = LG[:, i % 2, s["off"]:s["off"] + s["n"]]
                        if "slope" in s:
                            ins = v.scalar_tensor_tensor(dst, s["bias"], s["slope"], bank(s["bank"], s["n"]),
                                                         ALU.mult, ALU.add)
                        else:
                            ins = v.scalar_tensor_tensor(dst, bank(s["bank"], s["n"]), HD ** -0.5, s["bias"],
                                                         ALU.mult, ALU.add)
                    ins.then_inc(lg_read, 1)
                    dve.wait_ge(lg_read, first + i + 1)
                    order(v.reduce_max(mx, LG[:, i % 2, 0:it["n"]], AX.X))
                    if "sink" in it:
                        order(v.tensor_tensor(mx, mx, SNK[:, it["sink"]:it["sink"] + 1], ALU.max))
                    v.tensor_scalar(nmx, mx, -1.0, None, ALU.mult).then_inc(nmx_ready, 1)
                    dve.wait_ge(exp_ready, first + i + 1)
                    if "sink" in it:
                        order(v.tensor_tensor(total, total, es, ALU.add))
                    order(v.reciprocal(rec, total))
                    v.tensor_scalar(LG[:, i % 2, 0:it["n"]], LG[:, i % 2, 0:it["n"]], rec, None,
                                    ALU.mult).then_inc(prob_ready, 1)

            v.memset(RB[N_BUCKETS:N_BUCKETS + 1, :], NEG).then_inc(rb_ready, 1)
            dve.wait_ge(params_in, 16)
            dve.wait_ge(x_in, 16)
            normalise(0)
            split_transposed(0, "mix_pre")
            dve.wait_ge(toe_stored, 16)
            order(v.memset(LRAW[:, :, 0:1], 0.0))
            used(USE0["lora"])
            order(v.tensor_tensor(LTMP[:], LRAW[:, :, 0:T], LRAW[:, :, 1:T + 1], ALU.subtract))
            for c in range(2):
                last = v.scalar_tensor_tensor(LTMP[:, c, :], LTMP[:, c, :], pcol("mu", 24 + c), LRAW[:, c, 1:T + 1],
                                              ALU.mult, ALU.add)
            last.then_inc(lora_shifted, 1)
            dve.wait_ge(lora_act, 3)
            attention(att[0])
            dve.wait_ge(o_taken, len(items1))
            for h in range(2):
                order(v.memset(GM[h][:], 0.0))
            order(v.memset(RAW[:, :, :, 0:1], 0.0))
            dve.sem_inc(pair_open, 1)

            mask = C[:, CC["strict_incl"]:CC["strict_incl"] + 2 * P].bitcast(I32)

            def cast4(ap):
                return ap.unsqueeze(1).to_broadcast([P, NT, P])

            nl = len(LEVELS)
            as4 = lambda ap: ap.rearrange("p (t c) -> p t c", c=P)
            b3 = lambda b: as4(ps[:, b, :])

            def lmask(lv):
                return cast4(C[:, CC["levels"] + lv * P:CC["levels"] + (lv + 1) * P])

            def pairwise(q, off):
                def w(name, m, k):
                    dve.wait_ge(rs[name], q * (2 * m) + (m * off + k))
                return w

            def inc(ins, name):
                ins.then_inc(rs[name], 1)

            def col(name, q, off):
                return pcol_dyn(name, q * 2 + off) if not isinstance(q, int) else pcol(name, q * 2 + off)

            def prep(q, off, step, o):
                w, par = pairwise(q, off), off % 2
                rr, kk_, vv = (RAW[:, par, j, 1:T + 1] for j in range(3))

                def shift(j):
                    f = RAW[:, par, j, 1:T + 1]
                    o(v.tensor_tensor(CS[:], RAW[:, par, j, 0:T], f, ALU.subtract))
                    o(v.scalar_tensor_tensor(f, CS[:], col("mu", q, 8 * j + off), f, ALU.mult, ALU.add))

                if step == 0:
                    dve.wait_ge(rkv_taken, q * 4 + (2 * off + 2))
                    shift(0)
                    shift(1)
                elif step == 1:
                    o(v.tensor_scalar(KK[:], kk_, col("k_k", q, off), None, ALU.mult))
                    inc(v.tensor_tensor(X2[:], KK[:], KK[:], ALU.mult), "sq_ready")
                    shift(2)
                elif step == 2:
                    w("sig_ready", 1, 1)
                    o(v.tensor_scalar(T1[:], Ab[:], -1.0, col("k_a", q, off), ALU.add, ALU.mult))
                    o(v.scalar_tensor_tensor(kk_, T1[:], 1.0, kk_, ALU.add, ALU.mult))
                    inc(v.scalar_tensor_tensor(T1[:], rr, col("r_k", q, off), kk_, ALU.mult, ALU.mult), "rk_ready")
                    w("ss_full", 1, 1)
                    inc(v.tensor_scalar(E[:], bank(3), L2_EPS2, None, ALU.max), "nrm_ready")
                    for t in range(NT):
                        ins = v.tensor_tensor_scan(CS[:, t * P:(t + 1) * P], ones, SZ[:, t * P:(t + 1) * P], 0.0,
                                                   ALU.mult, ALU.add)
                    o(ins)
                elif step == 3:
                    w("sqrt_ready", 1, 1)
                    o(v.reciprocal(E[:], E[:]))
                    o(v.tensor_tensor(KK[:], KK[:], E[:], ALU.mult))
                elif step == 4:
                    o(v.tensor_tensor(as4(E[:]), as4(CS[:]), as4(CS[:])[:, :, HD - 1:HD].to_broadcast([P, NT, P]),
                                      ALU.subtract))
                    w("bonus_full", 1, 1)
                    inc(v.tensor_tensor(T1[:], E[:], SZ[:], ALU.subtract), "csm_ready")
                elif step == 5:
                    o(v.tensor_tensor(Ab[:], Ab[:], KK[:], ALU.mult))
                    o(v.tensor_tensor(BON[par][:], bank(2), vv, ALU.mult))
                elif step == 6:
                    w("exps_ready", 1, 1)
                    v.tensor_tensor(LM[:, par, 1, 0:NT - 1], as4(E[:])[:, 0:NT - 1, P - 1], LM[:, par, 0, 1:NT],
                                    ALU.mult)
                    v.tensor_tensor(RA[par][:, :, 0, :], as4(rr), as4(E[:]), ALU.mult)
                    v.scalar_tensor_tensor(RA[par][:, :, 1, :], as4(KK[:]), -1.0, as4(T1[:]), ALU.mult, ALU.mult)
                else:
                    o(v.tensor_tensor(KB[:, 0, :], kk_, X2[:], ALU.mult))
                    inc(v.tensor_tensor(KB[:, 1, :], Ab[:], X2[:], ALU.mult), "rakb_ready")

            def level(q, off, lv):
                w = pairwise(q, off)
                if lv == 0:
                    for h in range(2):
                        w("m_ready", 2 * nl, h + 1)
                        v.tensor_tensor(TT[h][:], f32(Mb[h][:]), cast4(ident), ALU.add)
                        w("x_full", 2 * nl, h + 1)
                        inc(v.tensor_tensor(Tb[h][:], b3(4 + h), cast4(ident), ALU.add), "t2_ready")
                        w("t2_ready", 2, h + 1)
                        inc(v.tensor_tensor(Mb[h][:], GM[h][:, :, 3, :], lmask(1), ALU.mult), "m_ready")
                    return
                for h in range(2):
                    w("x_full", 2 * nl, 2 * lv + h + 1)
                    inc(v.tensor_tensor(Xb[h][:], b3(4 + h), cast4(ident), ALU.add), "x1_ready")
                if lv + 1 < nl:
                    for h in range(2):
                        inc(v.tensor_tensor(Mb[h][:], GM[h][:, :, 3, :], lmask(lv + 1), ALU.mult), "m_ready")

            def refine(q, off, ahead, o):
                w = pairwise(q, off)
                for h in range(2):
                    w("u_full", 2, h + 1)
                    inc(v.tensor_tensor(Xb[h][:], b3(4 + h), f32(Tb[h][:]), ALU.subtract), "e_ready")
                if ahead:
                    prep(q, off + 1, 4, o)
                for h in range(2):
                    w("c_full", 2, h + 1)
                    inc(v.tensor_tensor(TF[h][:], b3(6 + h), f32(TT[h][:]), ALU.add), "tf_ready")

            def chunks(q, off, ahead, o):
                w, par = pairwise(q, off), off % 2
                for t in range(NT):
                    w("sa_full", NT, t + 1)
                    inc(v.tensor_copy(SA[:], ps[:, 4, P:2 * P]), "sa_ready")
                    if t < NT - 1:
                        w("s_full", NT - 1, t + 1)
                        o(v.tensor_tensor(S[:], ps[:, 5, P:P + HD], S[:], ALU.add))
                        inc(v.tensor_scalar(S[:], S[:], LM[:, par, 1, t:t + 1], None, ALU.mult), "s_ready")
                        if ahead:
                            prep(q, off + 1, 5 + t, o)

            def norm_first(q, off, o):
                w = pairwise(q, off)
                w("mu_full", 1, 1)
                o(v.scalar_tensor_tensor(T1[:], bank(2), -1.0 / HD, E[:], ALU.mult, ALU.add))
                inc(v.tensor_tensor(X2[:], T1[:], T1[:], ALU.mult), "ysq_ready")

            def norm_second(q, off, o):
                w = pairwise(q, off)
                w("std_ready", 1, 1)
                o(v.reciprocal(X2[:], X2[:]))

            def norm_third(q, off, o):
                par = off % 2
                o(v.tensor_tensor(T1[:], T1[:], X2[:], ALU.mult))
                o(v.tensor_scalar(T1[:], T1[:], col("ln_w", q, off), col("ln_b", q, off), ALU.mult, ALU.add))
                o(v.tensor_tensor(T1[:], T1[:], BON[par][:], ALU.add))
                dst = ORW[:, q * 2 + off, :] if isinstance(q, int) else \
                    ORW[:, bass.ds(q * 2 + off, 1), :].rearrange("p a t -> p (a t)")
                v.tensor_tensor(dst, T1[:], Gb[par][:], ALU.mult).then_inc(pair_open, 1)
                dve.wait_ge(pair_open, q * 2 + (off + 2))

            def grams(q, off):
                w = pairwise(q, off)
                for t in range(NT):
                    w("gram_full", NT, t + 1)
                    v.memset(stat[:, 40 + 4 * (off % 2) + t:41 + 4 * (off % 2) + t], 0.0)
                    for h in range(2):
                        ins = v.copy_predicated(GM[h][:, t, :, :].rearrange("p (a b) c -> p a (b c)", a=2),
                                                mask.unsqueeze(1).to_broadcast([P, 2, 2 * P]),
                                                ps[:, 4 + 2 * (t % 2) + h, :].rearrange("p (a b) -> p a b", a=2))
                    inc(ins, "gram_taken")
                w("gram_taken", NT, NT)
                inc(v.memset(S[:], 0.0), "s_ready")
                for h in range(2):
                    inc(v.tensor_tensor(Mb[h][:], GM[h][:, :, 3, :], lmask(0), ALU.mult), "m_ready")

            def pair_step(q, off, ahead, o):
                for lv in range(3, nl):
                    level(q, off, lv)
                    if ahead:
                        prep(q, off + 1, lv - 3, o)
                refine(q, off, ahead, o)
                chunks(q, off, ahead, o)
                if ahead:
                    grams(q, off + 1)
                    level(q, off + 1, 0)
                norm_first(q, off, o)
                if ahead:
                    level(q, off + 1, 1)
                norm_second(q, off, o)
                if ahead:
                    level(q, off + 1, 2)
                norm_third(q, off, o)

            for step in range(8):
                prep(0, 0, step, order)
            grams(0, 0)
            for lv in range(3):
                level(0, 0, lv)
            with dve.Fori(0, PAIRS // 2 - 1) as q:
                o = Order(dve, dve_rwkv, q * DVE_STEPS)
                pair_step(q, 0, True, o)
                pair_step(q, 1, True, o)
                assert o.n == DVE_STEPS, o.n
            o = Order(dve, dve_rwkv, (PAIRS // 2 - 1) * DVE_STEPS)
            pair_step(PAIRS // 2 - 1, 0, True, o)
            pair_step(PAIRS // 2 - 1, 1, False, o)
            dve.wait_ge(pair_open, PAIRS + 1)

            dve.wait_ge(split_hi, 1)
            v.tensor_tensor(OAl[:], OAT[:], f32(OAh[:]), ALU.subtract).then_inc(split_lo, 1)
            dve.wait_ge(split_hi, 2)
            v.tensor_tensor(ORl[:], ORW[:], f32(ORh[:]), ALU.subtract).then_inc(split_lo, 1)

            def gate_times(name, uses, M, G=None, tmp=None):
                for u in range(uses):
                    d = USE0[name] + u
                    dve.wait_ge(pair_full, d + 1)
                    src = ps[:, 2 * (d % 2):2 * (d % 2) + 2, :]
                    m = M[:, 2 * u:2 * u + 2, :]
                    if G is None:
                        v.tensor_tensor(m, m, src, ALU.mult).then_inc(pair_taken[d % 2], 1)
                        dve.wait_ge(pair_taken[d % 2], d // 2 + 1)
                    else:
                        g = G[:, 2 * u:2 * u + 2, :]
                        v.tensor_tensor(g, g, src, ALU.mult).then_inc(pair_taken[d % 2], 1)
                        dve.wait_ge(pair_taken[d % 2], d // 2 + 1)
                        order(v.tensor_tensor(m, m, g, ALU.add))

            def merge_low(k, M):
                dve.sem_inc(merged_hi, 1)
                dve.wait_ge(merged_hi, 2 * k + 2)
                v.tensor_tensor(HTl[:], M[:], f32(HTh[:]), ALU.subtract).then_inc(merged_lo, 1)

            for d in (USE0["gate0"] + 2, USE0["gate0"] + 3):
                used(d)
            gate_times("attb", 4, MG)
            dve.wait_ge(gate_back, 16)
            gate_times("rwkvb", 4, MG, G=G1)
            merge_low(0, MG)
            dve.wait_ge(x_back, 16)
            add_normed(0)
            normalise(1)
            split_transposed(1, "ffn_pre")
            order(v.memset(Y[:], 0.0))

            def add_rows(i, j, rows0):
                if rows0 or not (isinstance(i, int) and 2 * i + j == 0):
                    dve.wait_ge(row_taken, i * (2 * NT) + (rows0 + NT * j))
                for tt in range(NT):
                    dve.wait_ge(row_full, i * (2 * NT) + (rows0 + NT * j + tt + 1))
                    b = 4 + 2 * (tt % 2)
                    v.tensor_tensor(Y[:, tt, :].rearrange("p (a b) -> p a b", a=2), ps[:, b:b + 2, :],
                                    Y[:, tt, :].rearrange("p (a b) -> p a b", a=2), ALU.add).then_inc(row_taken, 1)

            def hidden1(i, j):
                d = USE0["ffn"] + j
                dve.wait_ge(pair_taken[d % 2], i + (d // 2 + 1))
                if not (isinstance(i, int) and 2 * i + j == 0):
                    dve.wait_ge(hid_lo, i * 2 + j)
                v.tensor_tensor(HR2[:], HR[:], HR[:], ALU.mult).then_inc(hid_sq, 1)
                dve.wait_ge(hid_hi, i * 2 + (j + 1))
                v.tensor_tensor(HIl[:, j % 2, :, :], HR2[:], f32(HIh[:, j % 2, :, :]), ALU.subtract).then_inc(hid_lo, 1)

            hidden1(0, 0)
            hidden1(0, 1)
            add_rows(0, 0, 0)
            with dve.Fori(1, FF1_GROUPS // 2) as i:
                hidden1(i, 0)
                add_rows(i, -1, 0)
                hidden1(i, 1)
                add_rows(i, 0, 0)
            add_rows(FF1_GROUPS // 2 - 1, 1, 0)
            add_normed(1)
            normalise(2)
            split_transposed(2, "mix2")

            v.memset(Zp[:], 0.0).then_inc(kraw_ready, 1)
            order(v.memset(PW[:], 0.0))
            used(USE0["pool"])
            used(USE0["pool"] + 1)
            dve.wait_ge(ic_in, 16)
            a0, b0 = 8, 8 + T + 16
            for g in range(4):
                cur = Zp[:, g, :]
                for lvl in range(g + 1):
                    left, right = (1, 0) if lvl == 0 else (2 ** (lvl - 1), 2 ** (lvl - 1))
                    dst = PW[:, lvl % 2, :]
                    order(v.tensor_tensor(dst[:, a0:b0], cur[:, a0 - left:b0 - left], cur[:, a0 + right:b0 + right],
                                          ALU.add))
                    cur = dst
                mean = PW[:, (g + 1) % 2, 16:16 + T]
                order(v.tensor_tensor(mean, cur[:, 16:16 + T], IC[:, g, :], ALU.mult))
                order(v.tensor_tensor(mean, mean, Zp[:, g, 16:16 + T], ALU.subtract))
                order(v.tensor_copy(PDh[:, g, :], mean))
                v.tensor_tensor(PDl[:, g, :], mean, f32(PDh[:, g, :]), ALU.subtract).then_inc(pd_ready, 1)
                dve.wait_ge(pd_ready, g + 1)
            for u in range(2):
                d = USE0["group"] + u
                dve.wait_ge(split_hi, 3 + u)
                for c in range(2):
                    g = 2 * u + c
                    last = v.scalar_tensor_tensor(YPl[:, g, :], bank(2 * (d % 2) + c), pcol("pool_scale", g),
                                                  f32(YPh[:, g, :]), ALU.mult, ALU.subtract)
                last.then_inc(pair_taken[d % 2], 1)
            dve.wait_ge(sink_in, 16)
            attention(att[1])
            for d in (USE0["gatea"] + 2, USE0["gatea"] + 3):
                used(d)
            dve.wait_ge(split_hi, 5)
            v.tensor_tensor(O2l[:], O2[:], f32(O2h[:]), ALU.subtract).then_inc(split_lo, 1)
            gate_times("poolb", 4, MG2)
            gate_times("attnb", 4, MG2, G=G2)
            merge_low(1, MG2)
            for d in (USE0["wout2"] + 2, USE0["wout2"] + 3):
                used(d)
            v.tensor_tensor(Xr[:], Xr[:], Y[:], ALU.add).then_inc(x_ready, 1)
            dve.wait_ge(x_ready, 3)
            normalise(3)
            split_transposed(3, "ffn2")
            order(v.memset(Y[:], 0.0))
            R0 = NT * FF1_GROUPS

            def hidden2(i, j):
                d = USE0["ffn2"] + 2 * j
                dve.wait_ge(hid_raw, i * 2 + (j + 1))
                dve.wait_ge(hid_lo, i * 2 + (FF1_GROUPS + j))
                b = 2 * (d % 2)
                v.tensor_tensor(HR2[:], ps[:, b:b + 2, :], HR[:], ALU.mult).then_inc(pair_taken[d % 2], 1)
                dve.wait_ge(pair_taken[d % 2], i * 2 + (d // 2 + 1))
                d += 1
                dve.wait_ge(pair_full, i * 4 + (d + 1))
                b = 2 * (d % 2)
                v.tensor_tensor(HR2[:], ps[:, b:b + 2, :], HR2[:], ALU.mult).then_inc(pair_taken[d % 2], 1)
                dve.wait_ge(pair_taken[d % 2], i * 2 + (d // 2 + 1))
                dve.sem_inc(hid_sq, 1)
                dve.wait_ge(hid_hi, i * 2 + (FF1_GROUPS + j + 1))
                v.tensor_tensor(HIl[:, j % 2, :, :], HR2[:], f32(HIh[:, j % 2, :, :]), ALU.subtract).then_inc(hid_lo, 1)

            hidden2(0, 0)
            hidden2(0, 1)
            add_rows(0, 0, R0)
            with dve.Fori(1, FF2_GROUPS // 2) as i:
                hidden2(i, 0)
                add_rows(i, -1, R0)
                hidden2(i, 1)
                add_rows(i, 0, R0)
            i = FF2_GROUPS // 2
            hidden2(i, 0)
            add_rows(i, -1, R0)
            add_rows(i, 0, R0)
            dve.wait_ge(row_taken, NT * (FF1_GROUPS + FF2_GROUPS))
            v.tensor_tensor(Xr[:], Xr[:], Y[:], ALU.add).then_inc(x_ready, 1)
            dve.wait_ge(rms_ready, 5)
            dve.wait_ge(gain_in, 48)
            order(v.reciprocal(stat[:, 8:12], stat[:, 4:8]))
            for tt in range(NT):
                last = v.scalar_tensor_tensor(Y[:, tt, :], Xr[:, tt, :], stat[:, 8 + tt:9 + tt], GN[:],
                                              ALU.mult, ALU.mult)
            last.then_inc(y_ready, 1)


def kernel(**inputs):
    import concourse.bacc as _bacc
    from concourse.bass_utils import run_bass_kernel_spmd as _run

    a = {k: np.asarray(v) for k, v in inputs.items()}
    w_in, w_in2 = a["w_in"][0], a["w_in_2"][0]

    def unit(w, kts):
        u = np.ascontiguousarray(w.reshape(kts, P, -1).transpose(1, 0, 2)).reshape(P, -1)
        return u if u.shape[1] == UNIT else np.concatenate([u, np.zeros((P, UNIT - u.shape[1]), u.dtype)], 1)

    def cols(w, c0, n, step=256, kts=KT):
        return [unit(w[:, c:c + step], kts) for c in range(c0, c0 + n, step)]

    def grid(w):
        return [unit(w[r:r + 512, c:c + 512], 4) for c in (0, 512) for r in (0, 512)]

    def ffn(ups, down, groups):
        out = []
        for g in range(groups + 1):
            if g < groups:
                out += [unit(u[:, 256 * g:256 * g + 256], KT) for u in ups]
            if g > 0:
                out.append(unit(down[256 * (g - 1):256 * g], 2))
        return out

    rk0 = 3 * ATT_W
    gate0 = rk0 + 3 * RW + 256
    units = cols(w_in, 0, 2 * ATT_W) + cols(w_in, 2 * ATT_W, ATT_W) + cols(w_in, rk0 + 3 * RW, 256)
    for c in range(0, RW, P):
        units += [unit(np.concatenate([w_in[:, c0 + c:c0 + c + P] for c0 in two], 1), KT)
                  for two in ((rk0, rk0 + RW), (rk0 + 2 * RW, gate0 + D))]
    units += cols(w_in, gate0, D) + [unit(a["w_att_branch"][0], 2)] + cols(a["w_rwkv_branch"][0], 0, D)
    units += grid(a["w_out"][0]) + ffn([a["w_ffn1"][0]], a["w_ffn2"][0], FF1_GROUPS)
    units += cols(w_in2, 0, 512) + cols(w_in2, 512, 512) + cols(w_in2, 1024, 256)
    units += [unit(a["w_pool_group_2"][0].reshape(512, P), 4)]
    units += cols(w_in2, 1280, 2 * D)
    units += cols(a["w_pool_branch_2"][0], 0, D, 512, 4) + cols(a["w_attn_branch_2"][0], 0, D, 512, 4)
    units += grid(a["w_out_2"][0])
    units += ffn([a["w_ffn_gate_2"][0], a["w_ffn_up_2"][0]], a["w_ffn_down_2"][0], FF2_GROUPS)
    assert len(units) == N_UNITS, (len(units), N_UNITS)

    table = {"mu": "shift_mu", "w0": "w0", "a0": "a0", "k_k": "k_k", "k_a": "k_a", "r_k": "r_k", "ln_w": "ln_x_w",
             "ln_b": "ln_x_b", "b_gate": "b_gate", "mix_pre": "norm_mix_pre", "ffn_pre": "norm_ffn_pre",
             "mix2": "norm_mix_2", "ffn2": "norm_ffn_2", "pool_scale": "pool_scale_2"}
    params = np.concatenate([a[table[n]].reshape(-1, P) for n, _ in PCOLS]).T
    gains = np.stack([a["norm_mix_post"][0], a["norm_ffn_post"][0], a["norm_final_2"]])
    arrays = {
        "x": a["x"][0],
        "wpack": np.stack(units),
        "lora_wa": np.concatenate([a["w_w2"][0], a["w_a2"][0]]),
        "lora_g": a["w_g2"][0],
        "params": params,
        "rel_bias": a["rel_bias"],
        "post_gains": np.broadcast_to(gains[:, None, :], (3, P, D)),
        "sink": np.broadcast_to(a["sink_2"][0][None, :], (P, Q_HEADS2)),
        "ctab": constants(),
        "btab": bucket_table(),
        "icount": np.broadcast_to(inv_counts().reshape(1, -1), (P, 4 * T)),
    }
    nc = _bacc.Bacc("TRN2", target_bir_lowering=False, num_devices=1)
    feeds, args = {}, []
    for name, arr in arrays.items():
        arr = np.ascontiguousarray(arr)
        feeds[f"in_{name}"] = arr
        args.append(nc.dram_tensor(f"in_{name}", arr.shape, mybir.dt.from_np(arr.dtype), kind="ExternalInput").ap())
    args.append(nc.dram_tensor("out_x", (T, D), F32, kind="ExternalOutput").ap())
    build(nc, *args)
    r = _run(nc, [feeds], core_ids=[0])
    return r.results[0]["out_x"].reshape(1, T, D)
```
